# Optimizing a Trainium2 kernel written in Bass

```python
import math
import jax, jax.numpy as jnp
from jax import lax
import numpy as np

D_MODEL = 2048
BATCH = 1
SEQ = 512
DEPTH = 1

N_MIXERS = 4
N_SWA = (DEPTH + 3) // N_MIXERS
N_RWKV = (DEPTH + 2) // N_MIXERS
N_MLSTM = (DEPTH + 1) // N_MIXERS
N_FOX = DEPTH // N_MIXERS

SWA_HEAD_DIM = 64
SWA_HEADS = D_MODEL // SWA_HEAD_DIM
SWA_KV_HEADS = SWA_HEADS // 8
SWA_GROUP = SWA_HEADS // SWA_KV_HEADS
SWA_WIDTH = SWA_HEADS * SWA_HEAD_DIM
SWA_KV_WIDTH = SWA_KV_HEADS * SWA_HEAD_DIM
SWA_IN = 2 * SWA_WIDTH + 2 * SWA_KV_WIDTH
SWA_WINDOW = 128
SWA_BLOCK = 128
REL_BUCKETS = 32
REL_MAX_DIST = 128
RWKV_HEAD_DIM = 64
RWKV_HEADS = D_MODEL // RWKV_HEAD_DIM
RWKV_DECAY_LORA = 96
RWKV_AAA_LORA = 96
RWKV_N_MIX = 6
MLSTM_HEADS = 8
MLSTM_V_DIM = D_MODEL // MLSTM_HEADS
MLSTM_QK_DIM = MLSTM_V_DIM // 2
MLSTM_QK_WIDTH = MLSTM_HEADS * MLSTM_QK_DIM
MLSTM_V_WIDTH = MLSTM_HEADS * MLSTM_V_DIM
MLSTM_IN = 2 * MLSTM_QK_WIDTH + 3 * MLSTM_V_WIDTH + 2 * MLSTM_HEADS
MLSTM_CHUNK = 128
FOX_HEAD_DIM = 64
FOX_HEADS = D_MODEL // FOX_HEAD_DIM
FOX_WIDTH = FOX_HEADS * FOX_HEAD_DIM
FOX_IN = 4 * FOX_WIDTH + FOX_HEADS
FOX_BLOCK = 128

RMS_EPS = 1e-6
GN_EPS = 64e-5


def rms_norm(x, g):
    xf = x.astype(jnp.float32)
    y = xf * lax.rsqrt(jnp.mean(xf * xf, axis=-1, keepdims=True) + RMS_EPS)
    return (y * g.astype(jnp.float32)).astype(x.dtype)

def t5_bucket(dist):
    max_exact = REL_BUCKETS // 2
    d_f = jnp.maximum(dist, 1).astype(jnp.float32)
    large = max_exact + (jnp.log(d_f / max_exact) / math.log(REL_MAX_DIST / max_exact)
                         * (REL_BUCKETS - max_exact)).astype(jnp.int32)
    large = jnp.minimum(large, REL_BUCKETS - 1)
    return jnp.where(dist < max_exact, dist, large)

def swa_sink_mixer(h, w_in, q_gain, k_gain, sinks, rel_table, w_out):
    bsz, seq, _ = h.shape
    L = SWA_BLOCK
    nb = seq // L
    q, k, v, gate = jnp.split(h @ w_in, [SWA_WIDTH, SWA_WIDTH + SWA_KV_WIDTH,
                                         SWA_WIDTH + 2 * SWA_KV_WIDTH], axis=-1)
    q = rms_norm(q.reshape(bsz, seq, SWA_KV_HEADS, SWA_GROUP, SWA_HEAD_DIM), q_gain)
    k = rms_norm(k.reshape(bsz, seq, SWA_KV_HEADS, SWA_HEAD_DIM), k_gain)
    v = v.reshape(bsz, seq, SWA_KV_HEADS, SWA_HEAD_DIM)
    pad = ((0, 0), (L, 0), (0, 0), (0, 0))
    k_pad = jnp.pad(k, pad)
    v_pad = jnp.pad(v, pad)
    qi = jnp.arange(L)[:, None]
    kj = jnp.arange(2 * L)[None, :]
    dist = qi + L - kj
    in_band = (dist >= 0) & (dist < SWA_WINDOW)
    bias = rel_table.astype(jnp.float32)[t5_bucket(jnp.maximum(dist, 0))]
    bias = bias.transpose(2, 0, 1).reshape(SWA_KV_HEADS, SWA_GROUP, L, 2 * L)
    sink = sinks.astype(jnp.float32).reshape(SWA_KV_HEADS, SWA_GROUP, 1, 1)
    scale = SWA_HEAD_DIM ** -0.5
    q_blocks = q.reshape(bsz, nb, L, SWA_KV_HEADS, SWA_GROUP, SWA_HEAD_DIM).transpose(1, 0, 2, 3, 4, 5)

    def one_block(args):
        j, qj = args
        start = j * L
        kb = lax.dynamic_slice_in_dim(k_pad, start, 2 * L, axis=1)
        vb = lax.dynamic_slice_in_dim(v_pad, start, 2 * L, axis=1)
        s = jnp.einsum('bqhgd,bkhd->bhgqk', qj, kb).astype(jnp.float32) * scale + bias
        valid = in_band & (start - L + kj >= 0)
        s = jnp.where(valid, s, -jnp.inf)
        m = jnp.maximum(jnp.max(s, axis=-1, keepdims=True), sink)
        p = jnp.exp(s - m)
        p = p / (jnp.sum(p, axis=-1, keepdims=True) + jnp.exp(sink - m))
        return jnp.einsum('bhgqk,bkhd->bqhgd', p.astype(vb.dtype), vb)

    o = lax.map(one_block, (jnp.arange(nb), q_blocks))
    o = o.transpose(1, 0, 2, 3, 4, 5).reshape(bsz, seq, SWA_WIDTH)
    return (o * jax.nn.silu(gate)) @ w_out

def rwkv7_mixer(h, mix, w_in, w0, w_lora1, w_lora2, a0, a_lora1, a_lora2,
                k_k, k_a, r_k, gn_w, gn_b, w_out):
    bsz, seq, d = h.shape
    H, N = RWKV_HEADS, RWKV_HEAD_DIM
    f32 = jnp.float32
    xx = jnp.pad(h, ((0, 0), (1, 0), (0, 0)))[:, :-1] - h
    xm = h[None] + xx[None] * mix[:, None, None, :]
    r, k, v, g = jnp.einsum('cbsd,cde->cbse', xm[:4], w_in)
    w_pre = (w0 + jnp.tanh(xm[4] @ w_lora1) @ w_lora2).astype(f32)
    log_w = -jnp.exp(-jax.nn.softplus(-w_pre) - 0.5)
    a = jax.nn.sigmoid((a0 + (xm[5] @ a_lora1) @ a_lora2).astype(f32))

    def heads(t):
        return t.astype(f32).reshape(bsz, seq, H, N)

    r, k, v, a, log_w = heads(r), heads(k), heads(v), heads(a), heads(log_w)
    kk = k * k_k.astype(f32).reshape(H, N)
    kk = kk / jnp.maximum(jnp.sqrt(jnp.sum(kk * kk, axis=-1, keepdims=True)), 1e-12)
    k = k * (1.0 + (a - 1.0) * k_a.astype(f32).reshape(H, N))

    def step(state, inp):
        r_t, w_t, k_t, v_t, kk_t, a_t = inp
        sa = jnp.einsum('bhvk,bhk->bhv', state, -kk_t)
        state = (state * w_t[:, :, None, :]
                 + sa[..., None] * (kk_t * a_t)[:, :, None, :]
                 + v_t[..., None] * k_t[:, :, None, :])
        return state, jnp.einsum('bhvk,bhk->bhv', state, r_t)

    def tm(t):
        return t.transpose(1, 0, 2, 3)

    state0 = jnp.zeros((bsz, H, N, N), f32)
    _, y = lax.scan(step, state0, (tm(r), tm(jnp.exp(log_w)), tm(k), tm(v), tm(kk), tm(a)))
    y = tm(y)
    mu = jnp.mean(y, axis=-1, keepdims=True)
    var = jnp.mean(jnp.square(y - mu), axis=-1, keepdims=True)
    y = ((y - mu) * lax.rsqrt(var + GN_EPS)).reshape(bsz, seq, d) * gn_w + gn_b
    bonus = jnp.sum(r * k * r_k.astype(f32), axis=-1, keepdims=True) * v
    y = y + bonus.reshape(bsz, seq, d)
    return (y.astype(h.dtype) * jax.nn.silu(g)) @ w_out

def mlstm_mixer(h, w_in, b_i, b_f, h_gain, w_out):
    bsz, seq, _ = h.shape
    H, dk, dv, L = MLSTM_HEADS, MLSTM_QK_DIM, MLSTM_V_DIM, MLSTM_CHUNK
    nc = seq // L
    f32 = jnp.float32
    s1 = MLSTM_QK_WIDTH
    s2 = s1 + MLSTM_QK_WIDTH
    s3 = s2 + MLSTM_V_WIDTH
    s4 = s3 + MLSTM_V_WIDTH
    s5 = s4 + MLSTM_V_WIDTH
    s6 = s5 + H
    q, k, v, o_pre, gate, i_pre, f_pre = jnp.split(h @ w_in, [s1, s2, s3, s4, s5, s6], axis=-1)
    q = q.astype(f32).reshape(bsz, seq, H, dk) * dk ** -0.5
    k = k.astype(f32).reshape(bsz, seq, H, dk)
    v = v.astype(f32).reshape(bsz, seq, H, dv)
    i_log = (i_pre + b_i).astype(f32)
    f_log = jax.nn.log_sigmoid((f_pre + b_f).astype(f32))

    def chunks(t):
        t = t.reshape((bsz, nc, L) + t.shape[2:])
        return jnp.moveaxis(t, (1, 3), (0, 2))

    tri = jnp.tril(jnp.ones((L, L), dtype=bool))

    def chunk_step(carry, inp):
        C, n, m = carry
        qc, kc, vc, ic, fc = inp
        b = jnp.cumsum(fc, axis=-1)
        g = b[..., -1]
        dmat = jnp.where(tri, b[..., :, None] - b[..., None, :] + ic[..., None, :], -jnp.inf)
        inter = b + m[..., None]
        m_t = jnp.maximum(inter, jnp.max(dmat, axis=-1))
        w_intra = jnp.exp(dmat - m_t[..., None])
        w_inter = jnp.exp(inter - m_t)
        sw = jnp.einsum('bhtd,bhsd->bhts', qc, kc) * w_intra
        num = (w_inter[..., None] * jnp.einsum('bhvk,bhtk->bhtv', C, qc)
               + jnp.einsum('bhts,bhsv->bhtv', sw, vc))
        den = w_inter * jnp.einsum('bhk,bhtk->bht', n, qc) + jnp.sum(sw, axis=-1)
        h_t = num / jnp.maximum(jnp.abs(den), jnp.exp(-m_t))[..., None]
        decay_s = g[..., None] - b + ic
        m_new = jnp.maximum(g + m, jnp.max(decay_s, axis=-1))
        ws = jnp.exp(decay_s - m_new[..., None])
        carry_scale = jnp.exp(g + m - m_new)
        C = carry_scale[..., None, None] * C + jnp.einsum('bhs,bhsv,bhsk->bhvk', ws, vc, kc)
        n = carry_scale[..., None] * n + jnp.einsum('bhs,bhsk->bhk', ws, kc)
        return (C, n, m_new), h_t

    carry0 = (jnp.zeros((bsz, H, dv, dk), f32), jnp.zeros((bsz, H, dk), f32), jnp.zeros((bsz, H), f32))
    _, hs = lax.scan(chunk_step, carry0, (chunks(q), chunks(k), chunks(v), chunks(i_log), chunks(f_log)))
    hs = jnp.moveaxis(hs, (0, 2), (1, 3)).reshape(bsz, seq, H, dv)
    hs = rms_norm(hs, h_gain).reshape(bsz, seq, MLSTM_V_WIDTH).astype(h.dtype)
    return (hs * jax.nn.sigmoid(o_pre) * jax.nn.silu(gate)) @ w_out

def fox_mixer(h, w_in, b_f, q_gain, k_gain, w_out):
    bsz, seq, _ = h.shape
    H, dh, L = FOX_HEADS, FOX_HEAD_DIM, FOX_BLOCK
    nb = seq // L
    W = FOX_WIDTH
    q, k, v, gate, f_pre = jnp.split(h @ w_in, [W, 2 * W, 3 * W, 4 * W], axis=-1)
    q = rms_norm(q.reshape(bsz, seq, H, dh), q_gain)
    k = rms_norm(k.reshape(bsz, seq, H, dh), k_gain)
    v = v.reshape(bsz, seq, H, dh)
    log_f = jax.nn.log_sigmoid((f_pre + b_f).astype(jnp.float32))
    F = jnp.cumsum(log_f, axis=1).transpose(0, 2, 1)
    q_blocks = q.reshape(bsz, nb, L, H, dh).transpose(1, 0, 2, 3, 4)
    F_blocks = F.reshape(bsz, H, nb, L).transpose(2, 0, 1, 3)
    key_pos = jnp.arange(seq)
    scale = dh ** -0.5

    def one_block(args):
        j, qj, Fj = args
        s = (jnp.einsum('bqhd,bkhd->bhqk', qj, k).astype(jnp.float32) * scale
             + (Fj[..., :, None] - F[:, :, None, :]))
        q_pos = j * L + jnp.arange(L)
        s = jnp.where(key_pos[None, :] <= q_pos[:, None], s, -jnp.inf)
        p = jax.nn.softmax(s, axis=-1)
        return jnp.einsum('bhqk,bkhd->bqhd', p.astype(v.dtype), v)

    o = lax.map(one_block, (jnp.arange(nb), q_blocks, F_blocks))
    o = o.transpose(1, 0, 2, 3, 4).reshape(bsz, seq, W)
    return (o * jax.nn.silu(gate)) @ w_out

def first_inputs(seed: int = 0) -> dict:
    key = jax.random.key(seed)
    keys = jax.random.split(key, 48)
    counter = [0]

    def next_key():
        kk = keys[counter[0]]
        counter[0] += 1
        return kk

    def nrm(shape, scale):
        return jax.random.normal(next_key(), shape, jnp.float32) * scale

    def gain(shape):
        return 1.0 + nrm(shape, 0.05)

    D = D_MODEL
    return {
        "x": nrm((BATCH, SEQ, D), 1.0),
        "rel_bias": nrm((REL_BUCKETS, SWA_HEADS), 0.2),
        "swa_norm": gain((N_SWA, D)),
        "swa_w_in": nrm((N_SWA, D, SWA_IN), D ** -0.5),
        "swa_q_gain": gain((N_SWA, SWA_HEAD_DIM)),
        "swa_k_gain": gain((N_SWA, SWA_HEAD_DIM)),
        "swa_sinks": nrm((N_SWA, SWA_HEADS), 0.5),
        "swa_w_out": nrm((N_SWA, SWA_WIDTH, D), SWA_WIDTH ** -0.5),
        "rwkv_norm": gain((N_RWKV, D)),
        "rwkv_mix": jax.random.uniform(next_key(), (N_RWKV, RWKV_N_MIX, D), jnp.float32),
        "rwkv_w_in": nrm((N_RWKV, 4, D, D), D ** -0.5),
        "rwkv_w0": -2.0 + nrm((N_RWKV, D), 1.0),
        "rwkv_w_lora1": nrm((N_RWKV, D, RWKV_DECAY_LORA), D ** -0.5),
        "rwkv_w_lora2": nrm((N_RWKV, RWKV_DECAY_LORA, D), 0.5 * RWKV_DECAY_LORA ** -0.5),
        "rwkv_a0": nrm((N_RWKV, D), 0.1),
        "rwkv_a_lora1": nrm((N_RWKV, D, RWKV_AAA_LORA), D ** -0.5),
        "rwkv_a_lora2": nrm((N_RWKV, RWKV_AAA_LORA, D), 0.5 * RWKV_AAA_LORA ** -0.5),
        "rwkv_k_k": 0.85 + nrm((N_RWKV, D), 0.05),
        "rwkv_k_a": 1.0 + nrm((N_RWKV, D), 0.05),
        "rwkv_r_k": nrm((N_RWKV, RWKV_HEADS, RWKV_HEAD_DIM), 0.1),
        "rwkv_gn_w": gain((N_RWKV, D)),
        "rwkv_gn_b": nrm((N_RWKV, D), 0.02),
        "rwkv_w_out": nrm((N_RWKV, D, D), D ** -0.5),
        "mlstm_norm": gain((N_MLSTM, D)),
        "mlstm_w_in": nrm((N_MLSTM, D, MLSTM_IN), D ** -0.5),
        "mlstm_b_i": nrm((N_MLSTM, MLSTM_HEADS), 0.1),
        "mlstm_b_f": 3.0 + nrm((N_MLSTM, MLSTM_HEADS), 0.5),
        "mlstm_h_gain": gain((N_MLSTM, MLSTM_HEADS, MLSTM_V_DIM)),
        "mlstm_w_out": nrm((N_MLSTM, MLSTM_V_WIDTH, D), MLSTM_V_WIDTH ** -0.5),
        "fox_norm": gain((N_FOX, D)),
        "fox_w_in": nrm((N_FOX, D, FOX_IN), D ** -0.5),
        "fox_b_f": 3.0 + nrm((N_FOX, FOX_HEADS), 0.5),
        "fox_q_gain": gain((N_FOX, FOX_HEAD_DIM)),
        "fox_k_gain": gain((N_FOX, FOX_HEAD_DIM)),
        "fox_w_out": nrm((N_FOX, FOX_WIDTH, D), FOX_WIDTH ** -0.5),
    }

def first_block(x, rel_bias, swa_norm, swa_w_in, swa_q_gain, swa_k_gain, swa_sinks, swa_w_out,
              rwkv_norm, rwkv_mix, rwkv_w_in, rwkv_w0, rwkv_w_lora1, rwkv_w_lora2, rwkv_a0,
              rwkv_a_lora1, rwkv_a_lora2, rwkv_k_k, rwkv_k_a, rwkv_r_k, rwkv_gn_w, rwkv_gn_b,
              rwkv_w_out, mlstm_norm, mlstm_w_in, mlstm_b_i, mlstm_b_f, mlstm_h_gain, mlstm_w_out,
              fox_norm, fox_w_in, fox_b_f, fox_q_gain, fox_k_gain, fox_w_out):
    for layer in range(DEPTH):
        kind, idx = layer % N_MIXERS, layer // N_MIXERS
        if kind == 0:
            x = x + swa_sink_mixer(rms_norm(x, swa_norm[idx]), swa_w_in[idx], swa_q_gain[idx],
                                   swa_k_gain[idx], swa_sinks[idx], rel_bias, swa_w_out[idx])
        elif kind == 1:
            x = x + rwkv7_mixer(rms_norm(x, rwkv_norm[idx]), rwkv_mix[idx], rwkv_w_in[idx],
                                rwkv_w0[idx], rwkv_w_lora1[idx], rwkv_w_lora2[idx], rwkv_a0[idx],
                                rwkv_a_lora1[idx], rwkv_a_lora2[idx], rwkv_k_k[idx], rwkv_k_a[idx],
                                rwkv_r_k[idx], rwkv_gn_w[idx], rwkv_gn_b[idx], rwkv_w_out[idx])
        elif kind == 2:
            x = x + mlstm_mixer(rms_norm(x, mlstm_norm[idx]), mlstm_w_in[idx], mlstm_b_i[idx],
                                mlstm_b_f[idx], mlstm_h_gain[idx], mlstm_w_out[idx])
        else:
            x = x + fox_mixer(rms_norm(x, fox_norm[idx]), fox_w_in[idx], fox_b_f[idx],
                              fox_q_gain[idx], fox_k_gain[idx], fox_w_out[idx])
    return x


N_META = 16
BLOCK_Q = 128
SB_HEADS = 8
SB_HEAD_DIM = 128
SB_WIDTH = SB_HEADS * SB_HEAD_DIM
DIFF_HEADS = 8
DIFF_QK_DIM = 64
DIFF_V_DIM = 2 * DIFF_QK_DIM
DIFF_QK_WIDTH = DIFF_HEADS * 2 * DIFF_QK_DIM
DIFF_WIDTH = DIFF_HEADS * DIFF_V_DIM
MIX_WIDTH = SB_WIDTH + DIFF_WIDTH
IN_SIZES = (SB_WIDTH, SB_WIDTH, SB_WIDTH, SB_WIDTH,
            DIFF_QK_WIDTH, DIFF_QK_WIDTH, DIFF_WIDTH, DIFF_WIDTH)
IN_WIDTH = 4 * SB_WIDTH + 2 * DIFF_QK_WIDTH + 2 * DIFF_WIDTH
ROPE_THETA = 500000.0
ROT_DIM = DIFF_QK_DIM // 4
SUBLN_EPS = 1e-5


def rms_norm_2(x, w, eps=RMS_EPS):
    xf = x.astype(jnp.float32)
    y = xf * lax.rsqrt(jnp.mean(xf * xf, axis=-1, keepdims=True) + eps)
    return (y * w.astype(jnp.float32)).astype(x.dtype)

def lambda_init_for(layer):
    return 0.8 - 0.6 * math.exp(-0.3 * layer)

def partial_rope(x, cos, sin):
    half = ROT_DIM // 2
    c = cos[None, :, None, None, :]
    s = sin[None, :, None, None, :]
    x1 = x[..., :half]
    x2 = x[..., half:ROT_DIM]
    return jnp.concatenate([x1 * c - x2 * s, x2 * c + x1 * s, x[..., ROT_DIM:]], axis=-1)

def stick_breaking_block(q, k, v, q_pos, k_pos):
    z = jnp.einsum('bhqd,bhkd->bhqk', q, k) / math.sqrt(q.shape[-1])
    mask = k_pos[None, :] < q_pos[:, None]
    log_beta = jax.nn.log_sigmoid(z)
    log_keep = jnp.where(mask, jax.nn.log_sigmoid(-z), 0.0)
    tail = lax.cumsum(log_keep, axis=3, reverse=True) - log_keep
    a = jnp.where(mask, jnp.exp(log_beta + tail), 0.0)
    return jnp.einsum('bhqk,bhkd->bhqd', a, v)

def diff_attention_block(q, k, v, lam, q_pos, k_pos):
    s = jnp.einsum('bhcqd,bhckd->bhcqk', q, k) / math.sqrt(q.shape[-1])
    mask = k_pos[None, :] <= q_pos[:, None]
    p = jax.nn.softmax(jnp.where(mask, s, -jnp.inf), axis=-1)
    w = p[:, :, 0] - lam * p[:, :, 1]
    return jnp.einsum('bhqk,bhkd->bhqd', w, v)

def second_inputs(seed: int = 0) -> dict:
    key = jax.random.key(seed)
    ks = jax.random.split(key, 13)
    f32 = jnp.float32
    x = jax.random.normal(ks[0], (BATCH, SEQ, D_MODEL), f32)
    meta = jax.random.normal(ks[1], (N_META, D_MODEL), f32)
    norm_w = 1.0 + 0.02 * jax.random.normal(ks[2], (DEPTH, D_MODEL), f32)
    w_in = jax.random.normal(ks[3], (DEPTH, D_MODEL, IN_WIDTH), f32) * D_MODEL ** -0.5
    q_norm_w = 1.0 + 0.02 * jax.random.normal(ks[4], (DEPTH, DIFF_QK_DIM), f32)
    k_norm_w = 1.0 + 0.02 * jax.random.normal(ks[5], (DEPTH, DIFF_QK_DIM), f32)
    lambda_q1 = 0.1 * jax.random.normal(ks[6], (DEPTH, DIFF_QK_DIM), f32)
    lambda_k1 = 0.1 * jax.random.normal(ks[7], (DEPTH, DIFF_QK_DIM), f32)
    lambda_q2 = 0.1 * jax.random.normal(ks[8], (DEPTH, DIFF_QK_DIM), f32)
    lambda_k2 = 0.1 * jax.random.normal(ks[9], (DEPTH, DIFF_QK_DIM), f32)
    subln_w = 1.0 + 0.02 * jax.random.normal(ks[10], (DEPTH, DIFF_V_DIM), f32)
    w_out = jax.random.normal(ks[11], (DEPTH, MIX_WIDTH, D_MODEL), f32) * MIX_WIDTH ** -0.5
    return {"x": x, "meta": meta, "norm_w": norm_w, "w_in": w_in,
            "q_norm_w": q_norm_w, "k_norm_w": k_norm_w,
            "lambda_q1": lambda_q1, "lambda_k1": lambda_k1,
            "lambda_q2": lambda_q2, "lambda_k2": lambda_k2,
            "subln_w": subln_w, "w_out": w_out}

def second_block(x, meta, norm_w, w_in, q_norm_w, k_norm_w, lambda_q1, lambda_k1,
              lambda_q2, lambda_k2, subln_w, w_out):
    f32 = jnp.float32
    b, seq = x.shape[0], x.shape[1]
    h = jnp.concatenate(
        [jnp.broadcast_to(meta[None].astype(x.dtype), (b, N_META, D_MODEL)), x], axis=1)
    t_all = h.shape[1]
    pos = jnp.arange(t_all, dtype=f32)
    inv_freq = ROPE_THETA ** (-jnp.arange(0, ROT_DIM, 2, dtype=f32) / ROT_DIM)
    ang = pos[:, None] * inv_freq[None, :]
    cos, sin = jnp.cos(ang), jnp.sin(ang)
    split_at = list(np.cumsum(IN_SIZES)[:-1])
    real_blocks = [(N_META + i * BLOCK_Q, N_META + (i + 1) * BLOCK_Q)
                   for i in range(seq // BLOCK_Q)]

    for l in range(DEPTH):
        last = l == DEPTH - 1
        q_start = N_META if last else 0
        blocks = ([] if last else [(0, N_META)]) + real_blocks
        lam_init = lambda_init_for(l)

        u = rms_norm_2(h, norm_w[l])
        proj = jnp.einsum('btd,de->bte', u, w_in[l])
        sb_q, sb_k, sb_v, sb_g, df_q, df_k, df_v, df_g = jnp.split(proj, split_at, axis=-1)

        def heads(t, n, d):
            return t.reshape(b, t.shape[1], n, d).transpose(0, 2, 1, 3).astype(f32)

        sbq = heads(sb_q[:, q_start:], SB_HEADS, SB_HEAD_DIM)
        sbk = heads(sb_k, SB_HEADS, SB_HEAD_DIM)
        sbv = heads(sb_v, SB_HEADS, SB_HEAD_DIM)

        dq = df_q.reshape(b, t_all, DIFF_HEADS, 2, DIFF_QK_DIM).astype(f32)
        dk = df_k.reshape(b, t_all, DIFF_HEADS, 2, DIFF_QK_DIM).astype(f32)
        dq = partial_rope(rms_norm_2(dq, q_norm_w[l]), cos, sin).transpose(0, 2, 3, 1, 4)
        dk = partial_rope(rms_norm_2(dk, k_norm_w[l]), cos, sin).transpose(0, 2, 3, 1, 4)
        dq = dq[:, :, :, q_start:]
        dv = heads(df_v, DIFF_HEADS, DIFF_V_DIM)
        lam = (jnp.exp(jnp.sum(lambda_q1[l].astype(f32) * lambda_k1[l].astype(f32)))
               - jnp.exp(jnp.sum(lambda_q2[l].astype(f32) * lambda_k2[l].astype(f32)))
               + lam_init)

        sb_outs, df_outs = [], []
        for (a, e) in blocks:
            q_pos = jnp.arange(a, e)
            k_pos = jnp.arange(e)
            qa, qe = a - q_start, e - q_start
            sb_outs.append(stick_breaking_block(
                sbq[:, :, qa:qe], sbk[:, :, :e], sbv[:, :, :e], q_pos, k_pos))
            df_outs.append(diff_attention_block(
                dq[:, :, :, qa:qe], dk[:, :, :, :e], dv[:, :, :e], lam, q_pos, k_pos))

        t_q = t_all - q_start
        sb_o = jnp.concatenate(sb_outs, axis=2).transpose(0, 2, 1, 3).reshape(b, t_q, SB_WIDTH)
        df_o = jnp.concatenate(df_outs, axis=2).transpose(0, 2, 1, 3)
        df_o = (rms_norm_2(df_o, subln_w[l], SUBLN_EPS) * (1.0 - lam_init)).reshape(b, t_q, DIFF_WIDTH)

        mixed = jnp.concatenate(
            [sb_o * jax.nn.silu(sb_g[:, q_start:].astype(f32)),
             df_o * jax.nn.silu(df_g[:, q_start:].astype(f32))], axis=-1).astype(h.dtype)
        y = jnp.einsum('bte,ed->btd', mixed, w_out[l])
        h = jnp.concatenate([h[:, :q_start], h[:, q_start:] + y], axis=1)

    return h[:, N_META:]


def setup_inputs(seed=0):
    out = dict(first_inputs(seed))
    for name, value in second_inputs(seed + 1).items():
        if name != "x":
            out[name + "_2"] = value
    return out


def reference(
    x, rel_bias, swa_norm, swa_w_in, swa_q_gain, swa_k_gain, swa_sinks, swa_w_out, rwkv_norm,
    rwkv_mix, rwkv_w_in, rwkv_w0, rwkv_w_lora1, rwkv_w_lora2, rwkv_a0, rwkv_a_lora1,
    rwkv_a_lora2, rwkv_k_k, rwkv_k_a, rwkv_r_k, rwkv_gn_w, rwkv_gn_b, rwkv_w_out, mlstm_norm,
    mlstm_w_in, mlstm_b_i, mlstm_b_f, mlstm_h_gain, mlstm_w_out, fox_norm, fox_w_in, fox_b_f,
    fox_q_gain, fox_k_gain, fox_w_out, meta_2, norm_w_2, w_in_2, q_norm_w_2, k_norm_w_2,
    lambda_q1_2, lambda_k1_2, lambda_q2_2, lambda_k2_2, subln_w_2, w_out_2,
):
    x = first_block(
        x, rel_bias, swa_norm, swa_w_in, swa_q_gain, swa_k_gain, swa_sinks, swa_w_out,
        rwkv_norm, rwkv_mix, rwkv_w_in, rwkv_w0, rwkv_w_lora1, rwkv_w_lora2, rwkv_a0,
        rwkv_a_lora1, rwkv_a_lora2, rwkv_k_k, rwkv_k_a, rwkv_r_k, rwkv_gn_w, rwkv_gn_b,
        rwkv_w_out, mlstm_norm, mlstm_w_in, mlstm_b_i, mlstm_b_f, mlstm_h_gain, mlstm_w_out,
        fox_norm, fox_w_in, fox_b_f, fox_q_gain, fox_k_gain, fox_w_out,
    )
    return second_block(
        x, meta_2, norm_w_2, w_in_2, q_norm_w_2, k_norm_w_2, lambda_q1_2, lambda_k1_2,
        lambda_q2_2, lambda_k2_2, subln_w_2, w_out_2,
    )


_drawn_inputs = setup_inputs


def setup_inputs(seed=0):
    import zlib

    import numpy as np

    out = dict(_drawn_inputs(seed))
    spreads = {}
    factors = {'swa_norm': 4.499,
     'swa_q_gain': 8.0,
     'swa_k_gain': 8.0,
     'swa_sinks': 8.0,
     'norm_w_2': 3.905,
     'q_norm_w_2': 8.0,
     'k_norm_w_2': 7.46,
     'lambda_q1_2': 4.056,
     'lambda_k1_2': 2.952,
     'subln_w_2': 8.0}
    for name, (base, spread) in spreads.items():
        noise = np.random.default_rng([zlib.crc32(name.encode()), seed]).standard_normal(out[name].shape)
        drawn = base * np.exp(spread * noise) if base else spread * noise
        out[name] = __import__('jax').numpy.asarray(drawn.astype(out[name].dtype))
    for name, factor in factors.items():
        out[name] = (out[name] * factor).astype(out[name].dtype)
    return out
```

```python
import math
from contextlib import ExitStack

import numpy as np

import concourse.bass as bass
from concourse import mybir

P = 128
TOK = 512
META = 16
ALL = META + TOK
D = 2048
KC = D // P
NB = TOK // P
QTR = KC // 4
POINTS = 8

HEADS, KV, HD = 32, 4, 64
SWA_K = HEADS * HD
SWA_V = SWA_K + KV * HD
SWA_GATE = SWA_V + KV * HD
UNITS = 4
BUCKETS, MAX_DIST = 32, 128
REL_COLS = 3 * P - 1
REL_PITCH = 4 * P

N2 = 8
SBH = 128
LAM_INIT = 0.8 - 0.6 * math.exp(-0.3 * 0)
ROT, THETA = 16, 500000.0
EPS, SUBLN_EPS = 1e-6, 1e-5
MASKED = -1e30

F32, F32R, BF16 = mybir.dt.float32, mybir.dt.float32r, mybir.dt.bfloat16
ALU, ACT = mybir.AluOpType, mybir.ActivationFunctionType
AX_X = mybir.AxisListType.X

TILES2 = [("dfq", 4096, (0,), False), ("dfk", 5120, (1, 2), True), ("dfv", 6144, (3, 0), True),
          ("dfg", 7168, (1,), False), ("sbq", 0, (2,), False), ("sbk", 1024, (3, 0), True),
          ("sbv", 2048, (1, 2), True), ("sbg", 3072, (3,), False)]
SBQ = 4
OWNERS2 = {"dfq": [("sbk", 1)], "dfk": [("sbv", 1)], "dfv": [("sbg", 1), ("dfq", 0)],
           "dfg": [("dfk", 0)], "sbq": [("dfk", 0)], "sbk": [("dfv", 0)],
           "sbv": [("dfg", 0), ("sbq", 0)], "sbg": [("sbk", 0)]}
T_KV, T_UNIT, T_OUT1, T_HEAD, T_OUT2, T_END = 0, 4, 36, 52, 116, 132


def shape_constants():
    f = np.float32
    eye = np.eye(P, dtype=f)
    head_ones = np.kron(np.eye(2), np.ones((HD, HD))).astype(f)
    ones = np.ones((P, P), f)
    k, m = np.meshgrid(np.arange(P), np.arange(P), indexing="ij")
    rot = np.zeros((P, P), f)
    for base in (0, HD):
        for d in range(ROT // 2):
            rot[base + d + ROT // 2, base + d] = 1
            rot[base + d, base + d + ROT // 2] = 1
    neg_tri = -(k >= m).astype(f)
    before = (k < m).astype(f)
    mats = np.stack([eye, head_ones, ones, rot, neg_tri, -ones, before])
    inv = (f(THETA) ** (-np.arange(0, ROT, 2, dtype=f) / f(ROT))).astype(f)
    ang = (np.arange(ALL, dtype=f)[:, None] * inv[None, :]).astype(f)
    cos, sin = np.ones((P, ALL), f), np.zeros((P, ALL), f)
    for base in (0, HD):
        for d in range(ROT // 2):
            cos[base + d] = cos[base + d + ROT // 2] = np.cos(ang[:, d])
            sin[base + d] = -np.sin(ang[:, d])
            sin[base + d + ROT // 2] = np.sin(ang[:, d])
    causal = np.zeros((P, ALL), f)
    causal[:, ALL - P:] = np.where(m <= k, 0, MASKED)
    strict = np.where(k < m, 0, MASKED).astype(f)
    dist = 2 * P - 1 - np.arange(REL_COLS)
    inside = (dist >= 0) & (dist < P)
    exact = BUCKETS // 2
    far = exact + (np.log(np.maximum(dist, 1).astype(f) / exact) / math.log(MAX_DIST / exact)
                   * (BUCKETS - exact)).astype(np.int32)
    bucket = np.where(dist < exact, dist, np.minimum(far, BUCKETS - 1))
    onehot = ((np.arange(BUCKETS)[:, None] == bucket[None]) & inside[None]).astype(f)
    outside = np.broadcast_to(np.where(inside, 0, MASKED).astype(f), (HEADS, REL_COLS))
    return {"c_mats": mats, "c_rope": np.stack([cos, sin]), "c_causal": causal, "c_strict": strict,
            "c_rel": np.stack([onehot, np.ascontiguousarray(outside)])}


def build(nc, x, rel_bias, norm1, w_in1, q_gain1, k_gain1, sinks, w_out1, meta, norm2, w_in2, q_gain2, k_gain2,
          lq1, lk1, lq2, lk2, subln, w_out2, c_mats, c_rope, c_causal, c_strict, c_rel, rel_rows, x1, out):
    with ExitStack() as ctx:
        def sb(name, shape, dt=F32, scope=ctx):
            return scope.enter_context(nc.sbuf_tensor(name, shape, dt))

        def sem(name):
            return ctx.enter_context(nc.semaphore(name))

        xh = sb("xh", [P, KC, ALL], F32R)
        xl = sb("xl", [P, KC, ALL], F32R)
        raw = sb("raw", [P, 2, KC, P])
        wh = sb("wh", [P, 2, KC, P], F32R)
        wl = sb("wl", [P, 2, KC, P], F32R)
        mixed = sb("mixed", [P, KC, TOK])
        rows = mixed[:, :, :].rearrange("p (t a) n -> p t (a n)", t=NB)
        mats = sb("mats", [P, 7, P])
        ident, head_ones, ones, rot, neg_tri, neg_ones, before = (mats[:, i, :] for i in range(7))
        gnorm = sb("gnorm", [P, 2, KC])
        gains = sb("gains", [P, 6])
        ssq = sb("ssq", [P, 2, NB + 1])
        rstd = sb("rstd", [P, 2, NB + 1])
        eps = sb("eps", [P, 2])
        chain_raw = sb("chain_raw", [P, ALL])
        chain_sq = sb("chain_sq", [P, ALL])
        chain_rs = sb("chain_rs", [P, ALL])
        gate_e = sb("gate_e", [P, TOK])
        shared = ExitStack()
        gate_raw = sb("gate_raw", [P, TOK], scope=shared)
        y_col = sb("y_col", [P, TOK], scope=shared)
        shared.close()
        lk_l = sb("lk_l", [P, TOK], F32R)
        later_h = sb("later_h", [P, TOK], F32R)

        one = ExitStack()
        relw = sb("relw", [BUCKETS, HEADS], scope=one)
        relc = sb("relc", [BUCKETS, 2, REL_COLS], scope=one)
        relb = sb("relb", [HEADS, REL_COLS], scope=one)
        sink = sb("sink", [P, 2, HEADS], scope=one)
        sink_u = sb("sink_u", [P, 2, 2, 2], scope=one)
        bias = sb("bias", [P, 2, 2, 2 * P], scope=one)
        kT1 = sb("kT1", [P, KV, TOK], scope=one)
        v1 = sb("v1", [P, KV, NB, HD], scope=one)
        qn = sb("qn", [P, TOK], scope=one)
        sg1 = sb("sg1", [P, TOK], scope=one)
        sc1 = sb("sc1", [P, 3, 2 * P], scope=one)
        p1 = sb("p1", [P, 4, 2 * P], scope=one)
        pT1 = sb("pT1", [P, 3, 2 * P], scope=one)
        st1 = sb("st1", [P, 8, 8], scope=one)
        one.close()

        two = ctx
        rope = sb("rope", [P, 2, ALL], scope=two)
        causal = sb("causal", [P, ALL], scope=two)
        strict = sb("strict", [P, P], scope=two)
        dfq = sb("dfq", [P, TOK], scope=two)
        dfk = sb("dfk", [P, ALL], scope=two)
        dfv = sb("dfv", [P, NB, P], scope=two)
        dfvm = sb("dfvm", [META, P], scope=two)
        dsg = sb("dsg", [P, TOK], scope=two)
        sbq = sb("sbq", [P, TOK], scope=two)
        sbk = sb("sbk", [P, ALL], scope=two)
        sbv = sb("sbv", [P, NB, P], scope=two)
        sbvm = sb("sbvm", [META, P], scope=two)
        ssg = sb("ssg", [P, TOK], scope=two)
        att = sb("att", [P, 6, ALL], scope=two)
        work = att[:, 0:2, :]
        prob = att[:, 2:4, :]
        wts = att[:, 4:6, :]
        metar = att[0:META, :, :].rearrange("p a n -> p (a n)")[:, 0:D]
        wmeta = sb("wmeta", [P, NB, META], scope=two)
        shared = ExitStack()
        pT2 = sb("pT2", [P, TOK], scope=shared)
        shared.close()
        lk_h = sb("lk_h", [P, TOK], F32R, scope=two)
        later = sb("later", [P, TOK], scope=two)
        later_l = sb("later_l", [P, TOK], F32R, scope=two)
        exact = sb("exact", [P, 4, P], F32R, scope=two)
        smeta = sb("smeta", [P, 2 * NB, META], scope=two)
        st2 = sb("st2", [P, 4, 2 * NB], scope=two)
        lamv = ssg[:, 0:4 * HD].rearrange("p (n d) -> p n d", n=4)
        lam = sb("lam", [P, 6], scope=two)

        def ps(name, shape):
            return ctx.enter_context(nc.psum_tensor(name, shape, F32))

        G = ps("G", [P, 4, TOK])
        S = ps("S", [P, 2, TOK])
        T = ps("T", [P, TOK])
        O = ps("O", [P, TOK])

        raw_in = [sem(f"raw_in{i}") for i in range(2)]
        q_in, sbq_in = sem("q_in"), sem("sbq_in")
        mats_in, c_in, m_in, x_in = sem("mats_in"), sem("c_in"), sem("m_in"), [sem(f"x_in{t}") for t in range(NB)]
        sets_ok = sem("sets_ok")
        w_hi, w_lo, tile_done = sem("w_hi"), sem("w_lo"), sem("tile_done")
        sq_done, rs_done, rows_done = sem("sq_done"), sem("rs_done"), sem("rows_done")
        t_done, x_hi, x_lo = sem("t_done"), sem("x_hi"), sem("x_lo")
        meta_rows, meta_t, meta_f, meta_hi, meta_lo = (
            sem(n) for n in ("meta_rows", "meta_t", "meta_f", "meta_hi", "meta_lo"))
        rel_mm, rel_ok, rel_out = sem("rel_mm"), sem("rel_ok"), sem("rel_out")
        sink_ok, sinku_ok, bias_in = sem("sink_ok"), sem("sinku_ok"), [sem(f"bias_in{i}") for i in range(2)]
        kv_raw, kv_stat, kv_ln, kv_rs, kv_n, kv_t, kv_v, kv_dup = (
            sem(n) for n in ("kv_raw", "kv_stat", "kv_ln", "kv_rs", "kv_n", "kv_t", "kv_v", "kv_dup"))
        q_raw, q_stat, q_ln, q_rs, q_ok = (sem(n) for n in ("q_raw", "q_stat", "q_ln", "q_rs", "q_ok"))
        g_act, g_mid, g_ok = sem("g_act"), sem("g_mid"), sem("g_ok")
        a_s, a_neg, a_exp, a_es, a_mid, a_p, a_t, a_pT, a_pv, a_out = (
            sem(n) for n in ("a_s", "a_neg", "a_exp", "a_es", "a_mid", "a_p", "a_t", "a_pT", "a_pv", "a_out"))
        split_hi, split_lo = sem("split_hi"), sem("split_lo")
        y_in, y_raw, y_t, y_sum, y_out = ([sem("y_in0"), sem("y_in1")], sem("y_raw"), sem("y_t"), sem("y_sum"),
                                          [sem("y_out0"), sem("y_out1")])
        lam_mid, lam_ok = sem("lam_mid"), sem("lam_ok")
        used = {n: sem("used_" + n) for n, *_ in TILES2}
        n_raw, n_stat, n_ln, n_rs, n_kn, n_rot, n_mid = (
            sem(n) for n in ("n_raw", "n_stat", "n_ln", "n_rs", "n_kn", "n_rot", "n_mid"))
        v_raw, v_t = sem("v_raw"), sem("v_t")
        e_gate, m_gate = sem("e_gate"), sem("m_gate")
        d_sm, d_smn, d_min, d_s, d_neg, d_exp, d_mid, d_w, d_t, d_pT, d_pv, d_tm, d_ptm, d_pvm = (
            sem("d_" + n) for n in ("sm", "smn", "min", "s", "neg", "exp", "mid", "w", "t", "pT", "pv", "tm",
                                    "ptm", "pvm"))
        d_sq, d_stat, d_ln, d_rs, d_norm, d_out = (sem("d_" + n) for n in ("sq", "stat", "ln", "rs", "norm", "out"))
        b_z, b_abs, b_e, b_ln, b_sp, b_lk, b_c, b_a, b_pv, b_zero, b_sum, b_kh, b_kl, b_lh, b_ll, b_out = (
            sem("b_" + n) for n in ("z", "abs", "e", "ln", "sp", "lk", "c", "a", "pv", "zero", "sum", "kh", "kl", "lh", "ll",
                                    "out"))
        exact_ok = sem("exact_ok")

        def after(eng, s, value):
            if not isinstance(value, int) or value > 0:
                eng.wait_ge(s, value)

        w1_v = w_in1.rearrange("(c p) n -> p c n", p=P)
        w2_v = w_in2.rearrange("(c p) n -> p c n", p=P)
        wo1_v = w_out1.rearrange("(c p) n -> p c n", p=P)
        wo2_v = w_out2.rearrange("(c p) n -> p c n", p=P)
        x_v = x.rearrange("(t p) n -> p t n", p=P)
        x1_v = x1.rearrange("(t p) n -> p t n", p=P)
        out_v = out.rearrange("(t p) n -> p t n", p=P)
        ds = bass.ds

        def window(i, g):
            return (i - 1, 3) if g == 0 else (i, g - 1)

        DF_S = {1 + 2 * n: n for n in range(2 * NB)}
        DF_T = {7 + 4 * j: j for j in range(NB)}
        DF_PV = {9 + 4 * j: j for j in range(NB)}
        DF_EXP = {2 + 2 * n: n for n in range(2 * NB)}
        DF_W = {5 + 4 * j: j for j in range(NB)}
        DF_PT = {8 + 4 * j: j for j in range(NB)}
        SB_Z = {1 + 4 * n: n for n in range(NB + 1)}
        SB_LK = {2 + 4 * n: n for n in range(NB + 1)}
        SB_C = {5 + 4 * n: n for n in range(NB + 1)}
        SB_SPLIT = {3 + 4 * n: n for n in range(NB + 1)}
        SB_LATER = {7 + 4 * n: n for n in range(NB)}
        SB_A = {6 + 4 * n: n for n in range(NB + 1)}
        SB_PV = {8 + 4 * n: n for n in range(NB + 1)}

        def sb_tile(n):
            if n < NB:
                t = NB - 1 - n
                return P, META + P * t, P * t
            return META, 0, 0

        block = ctx.enter_context(nc.Block())

        @block.sync
        def _(sp):
            def weights(tile, slot, w_v, col):
                after(sp, w_lo, 4 * (tile - 2) + 4)
                sp.dma_start(raw[:, slot, :, :], w_v[:, :, ds(col, P)]).then_inc(raw_in[slot], 16)

            for t in range(NB):
                sp.dma_start(rows[:, t, :], x_v[:, t, :]).then_inc(x_in[t], 16)
            sp.dma_start(mats[:, :, :], c_mats.rearrange("k p m -> p k m")).then_inc(mats_in, 16)
            sp.dma_start(gnorm[:, 0, :], norm1.rearrange("(c p) -> p c", p=P), allow_slow_non_contiguous=True).then_inc(mats_in, 16)

            for g in range(KV):
                after(sp, w_lo, 4 * (g - 2) + 4)
                for half, col in enumerate((SWA_K, SWA_V)):
                    sp.dma_start(raw[:, g % 2, :, HD * half:HD * half + HD],
                                 w1_v[:, :, col + HD * g:col + HD * g + HD]).then_inc(raw_in[g % 2], 16)
            sp.wait_ge(rel_ok, 1)
            sp.dma_start(bass.AP(tensor=rel_rows.tensor, offset=0,
                                 ap=[[P * REL_PITCH, HEADS], [REL_PITCH + 1, P], [1, REL_COLS]]),
                         relb[:, :].rearrange("h (a n) -> h a n", a=1).broadcast_to([HEADS, P, REL_COLS])).then_inc(rel_out, 16)
            sp.wait_ge(rel_out, 16)

            def unit_loads(i, g):
                u = 4 * i + g
                weights(T_UNIT + 2 * u, 0, w1_v, SWA_GATE + P * (4 * g + i))
                after(sp, a_neg, 8 * (u - 1))
                sp.dma_start(bias[:, g % 2, :, :],
                             rel_rows[ds((8 * g + 2 * i) * P, 2 * P), P - 1:3 * P - 1]
                             .rearrange("(h p) c -> p h c", p=P)).then_inc(bias_in[g % 2], 16)

            for g in range(KV):
                unit_loads(0, g)
            with sp.Fori(1, UNITS) as i:
                for g in range(KV):
                    unit_loads(i, g)

            def out_block(first, w_v, res_v, dst_v, base, chains, attention_over):
                def tile(i, half):
                    c = 2 * i + half
                    weights(first + c, half, w_v, P * c)
                    res, dst = chains[half]
                    if isinstance(c, int) and c == 0:
                        attention_over()
                    after(sp, y_sum, base + c - 1)
                    sp.dma_start(res, res_v[:, :, ds(P * c, P)]).then_inc(y_in[half], 16)

                def store(i, half):
                    c = 2 * i + half
                    res, dst = chains[half]
                    after(sp, y_sum, base + c + 1)
                    sp.dma_start(dst_v[:, :, ds(P * c, P)], dst if base else rows[:, :, ds(P * c, P)]).then_inc(y_out[half], 16)

                for half in range(2):
                    tile(0, half)
                with sp.Fori(1, KC // 2) as i:
                    for half in range(2):
                        tile(i, half)
                        store(i - 1, half)
                for half in range(2):
                    store(KC // 2 - 1, half)

            def chain_views():
                v = lambda b: b.rearrange("p (t n) -> p t n", t=NB)
                return [(v(chain_raw[:, 0:TOK]), v(gate_e[:, :])), (v(chain_sq[:, 0:TOK]), v(gate_raw[:, :]))]

            def head_load(h, ti):
                weights(T_HEAD + 8 * h + ti, ti % 2, w2_v, TILES2[ti][1] + P * h)

            out_block(T_OUT1, wo1_v, x_v, x1_v, 0, chain_views(), lambda: sp.wait_ge(a_out, 4 * UNITS))
            head_load(0, 0)
            head_load(0, 1)
            for half in range(2):
                sp.wait_ge(y_out[half], 16 * (KC // 2))
            sp.dma_start(metar[:, :], meta).then_inc(m_in, 16)
            sp.dma_start(rope[:, :, :], c_rope.rearrange("k p m -> p k m")).then_inc(m_in, 16)
            sp.dma_start(causal[:, :], c_causal).then_inc(m_in, 16)
            sp.dma_start(strict[:, :], c_strict).then_inc(m_in, 16)
            for n, v in enumerate((lq1, lk1, lq2, lk2)):
                sp.dma_start(lamv[:, n, :], v.rearrange("(a n) -> a n", a=1).broadcast_to([P, HD])).then_inc(m_in, 16)

            for ti in range(2, len(TILES2)):
                if ti != SBQ:
                    head_load(0, ti)
            with sp.Fori(1, N2) as h:
                for ti in range(len(TILES2)):
                    if ti != SBQ:
                        head_load(h, ti)

            def heads_over():
                sp.wait_ge(d_out, N2)
                sp.wait_ge(b_out, N2)

            out_block(T_OUT2, wo2_v, x1_v, out_v, KC, chain_views(), heads_over)
            for half in range(2):
                sp.wait_ge(y_out[half], 2 * 16 * (KC // 2))

        @block.gpsimd
        def _(pool):
            for col, g in enumerate((q_gain1, k_gain1, q_gain2, k_gain2)):
                for half in range(2):
                    pool.dma_start(gains[HD * half:HD * half + HD, col:col + 1],
                                   g.rearrange("(p a) -> p a", a=1)).then_inc(c_in, 16)
            pool.dma_start(gains[:, 4:5], subln.rearrange("(p a) -> p a", a=1)).then_inc(c_in, 16)
            pool.dma_start(sink[:, 1, :], sinks.rearrange("(a n) -> a n", a=1).broadcast_to([P, HEADS])).then_inc(c_in, 16)
            pool.dma_start(relw[:, :], rel_bias).then_inc(c_in, 16)
            pool.dma_start(relc[:, :, :], c_rel.rearrange("k p m -> p k m")).then_inc(c_in, 16)
            pool.dma_start(gnorm[:, 1, :], norm2.rearrange("(c p) -> p c", p=P), allow_slow_non_contiguous=True).then_inc(c_in, 16)

            def duplicate(g):
                pool.wait_ge(kv_n, g + 1)
                pool.dma_start(kT1[HD:P, g, :], kT1[0:HD, g, :]).then_inc(kv_dup, 16)

            def query_weights(i, g):
                after(pool, w_lo, 4 * (T_UNIT + 2 * (4 * i + g) - 1) + 4)
                pool.dma_start(raw[:, 1, :, :], w1_v[:, :, ds(P * (4 * g + i), P)]).then_inc(q_in, 16)

            for g in range(KV - 1):
                duplicate(g)
            query_weights(0, 0)
            duplicate(KV - 1)
            pool.wait_ge(sink_ok, 1)

            def sinks_of(i, g):
                u = 4 * i + g
                after(pool, a_es, 8 * (u - 1))
                pool.tensor_copy(sink_u[:, g % 2, :, :], sink[:, :, ds(8 * g + 2 * i, 2)]).then_inc(sinku_ok, 1)

            for g in range(KV):
                if g:
                    query_weights(0, g)
                sinks_of(0, g)
            with pool.Fori(1, UNITS) as i:
                for g in range(KV):
                    query_weights(i, g)
                    sinks_of(i, g)

            def sb_query_weights(h):
                after(pool, w_lo, 4 * (T_HEAD + 8 * h + SBQ - 2) + 4)
                pool.dma_start(raw[:, 0, :, :], w2_v[:, :, ds(P * h, P)]).then_inc(sbq_in, 16)

            sb_query_weights(0)
            with pool.Fori(1, N2) as h:
                sb_query_weights(h)

        @block.tensor
        def _(pe):
            def product(dst, slot, k, cols, last):
                for n, (w, v) in enumerate(((wh, xh), (wh, xl), (wl, xh))):
                    for d, (a, b) in zip(dst, cols):
                        mm = pe.matmul(d, w[:, slot, k, :], v[:, k, a:b], start=(k == 0 and n == 0),
                                       stop=(k == KC - 1 and n == 2))
                if last:
                    mm.then_inc(tile_done, 1)

            def gemm(tile, slot, dst, cols, at_point, chunk_ready=None):
                for k in range(KC):
                    if k % QTR == 0:
                        after(pe, w_lo, 4 * tile + k // QTR + 1)
                    if chunk_ready:
                        chunk_ready(k)
                    product(dst, slot, k, cols, k == KC - 1)
                    if k % 2:
                        at_point(k // 2)

            PLAIN = [(META, ALL)]
            SPLIT = [(0, ALL // 2), (ALL // 2, ALL)]

            def normalise(base):
                for c in range(KC):
                    if c >= 2:
                        pe.wait_ge(x_lo, base + c - 1)
                    for t in range(NB):
                        if c == 0:
                            pe.wait_ge(rows_done, base // KC * NB + t + 1)
                        mm = pe.transpose(S[:, c % 2, P * t:P * t + P], rows[:, t, P * c:P * c + P], ident)
                    mm.then_inc(t_done, 1)

            pe.wait_ge(mats_in, 16 * 2)
            normalise(0)
            pe.wait_ge(c_in, 16 * 13)
            pe.matmul(T[0:HEADS, 0:REL_COLS], relw[:, :], relc[:, 0, :], start=True, stop=True).then_inc(rel_mm, 1)

            def kv_stat_of(g):
                pe.wait_ge(kv_raw, 2 * g + 2)
                pe.matmul(G[:, g, :], head_ones, chain_sq[:, 0:TOK], start=True, stop=True).then_inc(kv_stat, 1)

            def kv_transpose(g):
                if g:
                    pe.wait_ge(kv_v, g)
                else:
                    pe.wait_ge(rel_ok, 1)
                for t in range(NB):
                    mm = pe.transpose(T[:, P * t:P * t + P], chain_raw[:, P * t:P * t + P], ident)
                mm.then_inc(kv_t, 1)

            for g in range(KV):
                def at_point(p, g=g):
                    if g and p == 1:
                        kv_stat_of(g - 1)
                    if g and p == 2:
                        kv_transpose(g - 1)
                gemm(T_KV + g, g % 2, [G[:, g, :]], PLAIN, at_point,
                     (lambda k: pe.wait_ge(x_lo, k + 1)) if g == 0 else None)

            def swa_scores(u, g, n):
                j, hh = n // 2, n % 2
                a, width = (0, P) if j == 0 else (P * (j - 1), 2 * P)
                if n == 0:
                    after(pe, q_ok, u + 1)
                    pe.wait_ge(kv_dup, 16 * KV)
                after(pe, a_neg, 8 * u + n - 1)
                lo, hi = HD * hh, HD * hh + HD
                pe.matmul(S[:, n % 2, 0:width], qn[lo:hi, P * j:P * j + P], kT1[lo:hi, g, a:a + width],
                          start=True, stop=True).then_inc(a_s, 1)

            def swa_transpose(u, n):
                if n == 0:
                    pe.wait_ge(kv_v, KV)
                after(pe, a_p, 8 * u + n + 1)
                after(pe, a_pT, 8 * u + n)
                for b in range(1 if n < 2 else 2):
                    mm = pe.transpose(T[:, P * b:P * b + P], p1[:, n % 4, P * b:P * b + P], ident)
                mm.then_inc(a_t, 1)

            def swa_values(u, g, n):
                j, hh = n // 2, n % 2
                after(pe, a_pT, 8 * u + n + 1)
                if n == 0:
                    after(pe, a_out, u)
                blocks = [0] if j == 0 else [j - 1, j]
                for s, b in enumerate(blocks):
                    mm = pe.matmul(O[HD * hh:HD * hh + HD, P * j:P * j + P], v1[:, g, b, :],
                                   pT1[:, n % 3, P * s:P * s + P], start=(s == 0), stop=(s == len(blocks) - 1))
                mm.then_inc(a_pv, 1)

            def swa_step(u, g, m):
                if m == 0:
                    after(pe, q_raw, 2 * u + 2)
                    pe.matmul(G[:, 2 * (g % 2) + 1, :], head_ones, chain_sq[:, 0:TOK], start=True,
                              stop=True).then_inc(q_stat, 1)
                if 0 <= m - 3 < 8:
                    swa_scores(u, g, m - 3)
                if 0 <= m - 6 < 8:
                    swa_transpose(u, m - 6)
                if 0 <= m - 7 < 8:
                    swa_values(u, g, m - 7)

            def swa_window(i, g, attend):
                u, gp = 4 * i + g, window(i, g)[1]

                def step(m):
                    if attend:
                        swa_step(u - 1, gp, m)
                    elif m in (1, 2):
                        (kv_stat_of if m == 1 else kv_transpose)(KV - 1)

                for half in range(2):
                    bank = 2 * (g % 2) + half
                    after(pe, q_ln if half else g_act, u - 1 if half else 2 * (u - 1))
                    if isinstance(u, int) and u < 2:
                        pe.wait_ge(kv_ln, 2 * u + half + 1)
                    gemm(T_UNIT + 2 * u + half, half, [G[:, bank, :]], PLAIN, lambda p: step(8 * half + p))

            for g in range(KV):
                swa_window(0, g, attend=g > 0)
            with pe.Fori(1, UNITS) as i:
                for g in range(KV):
                    swa_window(i, g, attend=True)
            for m in range(16):
                swa_step(4 * UNITS - 1, 3, m)

            def out_tile(first, base, i, half, split_base):
                c = 2 * i + half

                def transpose_before(p):
                    if p == 3 and not (isinstance(c, int) and c == 0):
                        after(pe, y_raw, base + c)
                        after(pe, y_sum, base + c - 1)
                        out_transpose(1 - half)

                after(pe, y_raw, base + c - 1)
                first_tile = isinstance(c, int) and c == 0
                if first_tile and base == 0:
                    pe.wait_ge(q_ln, 4 * UNITS)
                    pe.wait_ge(g_act, 8 * UNITS)
                    pe.wait_ge(a_pT, 8 * 4 * UNITS)
                elif first_tile:
                    pe.wait_ge(used["sbk"], N2)
                    pe.wait_ge(used["sbv"], N2)
                    pe.wait_ge(d_ln, N2)
                gemm(first + c, half, [G[:, half, :]], PLAIN, transpose_before,
                     (lambda k: pe.wait_ge(split_lo, split_base + k + 1)) if first_tile else None)

            def out_transpose(half):
                src = chain_rs if half else y_col
                for t in range(NB):
                    mm = pe.transpose(T[:, P * t:P * t + P], src[:, P * t:P * t + P], ident)
                mm.then_inc(y_t, 1)

            def out_block(first, base):
                for half in range(2):
                    out_tile(first, base, 0, half, base)
                with pe.Fori(1, KC // 2) as i:
                    for half in range(2):
                        out_tile(first, base, i, half, base)
                pe.wait_ge(y_raw, base + KC)
                pe.wait_ge(y_sum, base + KC - 1)
                out_transpose(1)

            out_block(T_OUT1, 0)

            normalise(KC)
            pe.wait_ge(meta_rows, 1)
            pe.wait_ge(y_sum, KC)
            for c in range(KC):
                mm = pe.transpose(T[:, META * c:META * c + META], metar[:, P * c:P * c + P], ident[0:META, 0:META])
            mm.then_inc(meta_t, 1)

            def banks(two):
                return [G[:, b, 0:(ALL // 2 if len(two) == 2 else TOK)] for b in two]

            def halves(buf, n):
                return [buf[:, 0:TOK]] if n == 1 else [buf[:, a:b] for a, b in SPLIT]

            def norm_stat(two, count):
                after(pe, n_raw, count)
                for d, s in zip(banks(two), halves(chain_sq, len(two))):
                    mm = pe.matmul(d, head_ones, s, start=True, stop=True)
                mm.then_inc(n_stat, 1)

            def rotate(two, count):
                after(pe, n_kn, count)
                for d, s in zip(banks(two), halves(dfq if len(two) == 1 else dfk, len(two))):
                    mm = pe.matmul(d, rot, s, start=True, stop=True)
                mm.then_inc(n_rot, 1)

            def value_rows(two, count):
                after(pe, v_raw, count)
                for t in range(NB):
                    pe.transpose(G[:, two[0], P * t:P * t + P], chain_raw[:, META + P * t:META + P * t + P], ident)
                pe.transpose(G[0:META, two[1], 0:P], chain_raw[:, 0:META], ident).then_inc(v_t, 1)

            def finish(h, ti, p):
                name, _, two, _ = TILES2[ti]
                if name in ("dfq", "dfk"):
                    if p == 1:
                        norm_stat(two, 2 * h + ti + 1)
                    if p == 5:
                        rotate(two, 2 * h + ti + 1)
                if name in ("dfv", "sbv") and p == 1:
                    value_rows(two, 2 * h + (1 if name == "dfv" else 2))

            def df_step(h, m):
                if m == 0:
                    after(pe, used["dfq"], h + 1)
                    after(pe, used["dfk"], h + 1)
                    after(pe, d_ln, h)
                    for c in range(2):
                        if c:
                            after(pe, d_sm, 2 * h + 1)
                        for j in range(NB):
                            n = 2 * j + c
                            mm = pe.matmul(T[:, META * n:META * n + META], dfq[HD * c:HD * c + HD, P * j:P * j + P],
                                           dfk[HD * c:HD * c + HD, 0:META], start=True, stop=True)
                        mm.then_inc(d_sm, 1)
                if m in DF_S:
                    n = DF_S[m]
                    j, c = n // 2, n % 2
                    after(pe, d_neg, 8 * h + n - 1)
                    if n < 2:
                        after(pe, b_a, 5 * h)
                    pe.matmul(S[:, n % 2, 0:P * (j + 1)], dfq[HD * c:HD * c + HD, P * j:P * j + P],
                              dfk[HD * c:HD * c + HD, META:META + P * (j + 1)], start=True, stop=True).then_inc(d_s, 1)
                if m in DF_T:
                    j = DF_T[m]
                    after(pe, d_w, 4 * h + j + 1)
                    after(pe, d_min, h + 1)
                    after(pe, d_pT, 4 * h + j)
                    for t in range(j + 1):
                        mm = pe.transpose(T[:, P * t:P * t + P], wts[:, j % 2, META + P * t:META + P * t + P], ident)
                    mm.then_inc(d_t, 1)
                if m in DF_PV:
                    j = DF_PV[m]
                    after(pe, d_pT, 4 * h + j + 1)
                    if j == 0:
                        after(pe, used["dfv"], h + 1)
                        after(pe, b_out, h)
                    for t in range(j + 1):
                        mm = pe.matmul(O[:, P * j:P * j + P], dfv[:, t, :], pT2[:, P * t:P * t + P],
                                       start=(j == 0 and t == 0), stop=False, skip_group_check=True)
                    mm.then_inc(d_pv, 1)
                if m == 22:
                    after(pe, d_pT, 4 * h + NB)
                    for j in range(NB):
                        mm = pe.transpose(T[0:META, P * j:P * j + P], wmeta[:, j, :], ident)
                    mm.then_inc(d_tm, 1)
                if m == 24:
                    after(pe, d_ptm, h + 1)
                    pe.matmul(O[:, :], dfvm[:, :], pT2[0:META, :], start=False, stop=True,
                              skip_group_check=True).then_inc(d_pvm, 1)
                if m == 27:
                    after(pe, d_sq, h + 1)
                    pe.matmul(T[:, :], ones, chain_sq[:, 0:TOK], start=True, stop=True).then_inc(d_stat, 1)

            def sb_step(h, m):
                if m in SB_Z:
                    n = SB_Z[m]
                    size, a, q = sb_tile(n)
                    if n == 0:
                        after(pe, used["sbk"], h + 1)
                        after(pe, used["sbq"], h + 1)
                    if n < 2:
                        after(pe, d_neg, 8 * h + 8)
                    else:
                        after(pe, b_a, 5 * h + n - 1)
                    pe.matmul(S[0:size, n % 2, 0:TOK - q], sbk[:, a:a + size], sbq[:, q:TOK], start=True,
                              stop=False, skip_group_check=True).then_inc(b_z, 1)
                if m in SB_C:
                    n = SB_C[m]
                    size, a, q = sb_tile(n)
                    z = S[0:size, n % 2, 0:TOK - q]
                    after(pe, b_kl, 5 * h + n + 1)
                    if n < NB:
                        pe.matmul(S[0:size, n % 2, 0:P], exact[:, 0, :], exact[:, 1, :], start=False, stop=False,
                                  skip_group_check=True)
                    if n:
                        after(pe, b_ll, 4 * h + n)
                        for part in (later_h, later_l):
                            pe.matmul(z, exact[:, 3, 0:size], part[:, q:TOK], start=False, stop=False,
                                      skip_group_check=True)
                    for part in (lk_h, lk_l):
                        mm = pe.matmul(z, exact[0:size, 2, 0:size], part[0:size, 0:TOK - q], start=False,
                                       stop=part is lk_l, skip_group_check=True)
                    mm.then_inc(b_c, 1)
                if m in SB_PV:
                    n = SB_PV[m]
                    size, a, q = sb_tile(n)
                    after(pe, b_a, 5 * h + n + 1)
                    if n == 0:
                        after(pe, used["sbv"], h + 1)
                        after(pe, d_out, h + 1)
                    v = sbv[:, NB - 1 - n, :] if n < NB else sbvm[:, :]
                    pe.matmul(O[:, q:TOK], v, prob[0:size, n % 2, 0:TOK - q], start=(n == 0), stop=(n == NB),
                              skip_group_check=True).then_inc(b_pv, 1)

            def head(h, attend):
                for ti, (name, _, two, with_meta) in enumerate(TILES2):
                    for owner, back in OWNERS2[name]:
                        after(pe, used[owner], h + 1 - back)

                    def at_point(p, ti=ti):
                        if ti:
                            finish(h, ti - 1, p)
                        if ti >= 4:
                            df_step(h, 8 * (ti - 4) + p)
                        elif attend:
                            sb_step(h - 1, 8 * ti + p)

                    first = isinstance(h, int) and h == 0 and ti == 0
                    if with_meta and isinstance(h, int) and h == 0 and ti == 1:
                        pe.wait_ge(meta_lo, 1)
                    gemm(T_HEAD + 8 * h + ti, ti % 2, banks(two), SPLIT if with_meta else PLAIN, at_point,
                         (lambda k: pe.wait_ge(x_lo, KC + k + 1)) if first else None)

            head(0, attend=False)
            pe.wait_ge(exact_ok, 4)
            with pe.Fori(1, N2) as h:
                head(h, attend=True)
            for m in range(32):
                sb_step(N2 - 1, m)
            out_block(T_OUT2, KC)

        @block.scalar
        def _(act):
            A = nc.scalar.activation

            KV_LOADS = 2 * 16 * (KV // 2)
            OUT1_LOADS = (KV_LOADS + 16 * 4 * UNITS, KV_LOADS)
            HEAD_LOADS = tuple(n + 16 * (KC // 2) for n in OUT1_LOADS)
            OUT2_LOADS = (HEAD_LOADS[0] + 3 * 16 * N2, HEAD_LOADS[1] + 4 * 16 * N2)

            def kv_loaded(g):
                return (raw_in[g % 2], 32 * (g // 2 + 1)) if g < KV else unit_loaded(0, 0)

            def unit_loaded(u, half):
                return (q_in, 16 * (u + 1)) if half else (raw_in[0], KV_LOADS + 16 * (u + 1))

            def out_loaded(loads, i, slot):
                return raw_in[slot], loads[slot] + 16 * (i + 1)

            def head_loaded(h, ti):
                if ti == SBQ:
                    return sbq_in, 16 * (h + 1)
                if ti % 2:
                    return raw_in[1], HEAD_LOADS[1] + 64 * h + 16 * (ti // 2 + 1)
                return raw_in[0], HEAD_LOADS[0] + 48 * h + 16 * (ti // 2 + (ti < SBQ))

            def split(pair, slot, quarter, loaded):
                if quarter == 0:
                    act.wait_ge(*loaded)
                    after(act, tile_done, 2 * pair + slot - 1)
                q = slice(QTR * quarter, QTR * quarter + QTR)
                A(wh[:, slot, q, :], raw[:, slot, q, :], ACT.Copy).then_inc(w_hi, 1)

            def row_sums(layer):
                junk = G[:, :, :].rearrange("p a b -> p (a b)")
                for t in range(NB + layer):
                    n = NB * layer + t
                    size = P if t < NB else META
                    if t < NB and layer == 0:
                        act.wait_ge(x_in[t], 16)
                    elif t < NB:
                        act.wait_ge(y_sum, KC)
                    else:
                        act.wait_ge(m_in, 16 * 8)
                    r = rstd[0:size, layer, t:t + 1]
                    A(junk[0:size, :], rows[:, t, :] if t < NB else metar, ACT.Square,
                      accum_out=ssq[0:size, layer, t:t + 1]).then_inc(sq_done, 1)
                    act.wait_ge(sq_done, n + 1)
                    A(r, ssq[0:size, layer, t:t + 1], ACT.Ln, bias=eps[0:size, 0:1], scale=1.0 / D).then_inc(rs_done, 1)
                    act.wait_ge(rs_done, 2 * n + 1)
                    A(r, r, ACT.Exp, scale=-0.5).then_inc(rs_done, 1)

            def normalised_hi(layer):
                for c in range(KC):
                    act.wait_ge(t_done, KC * layer + c + 1)
                    A(xh[:, c, META:ALL], S[:, c % 2, :], ACT.Copy, scale=gnorm[:, layer, c:c + 1]).then_inc(x_hi, 1)

            nc.scalar.preload_act_table_set("natural_log_exp_and_others")
            act.wait_ge(sets_ok, 1)
            row_sums(0)
            act.wait_ge(mats_in, 16 * 2)
            normalised_hi(0)
            for quarter in range(4):
                split(0, 0, quarter, kv_loaded(0))

            def kv_chain(g):
                act.wait_ge(tile_done, g + 1)
                after(act, kv_t, g)
                after(act, kv_n, g)
                A(chain_raw[:, 0:TOK], G[:, g, :], ACT.Copy).then_inc(kv_raw, 1)
                A(chain_sq[:, 0:TOK], G[:, g, :], ACT.Square).then_inc(kv_raw, 1)

            def kv_rstd(g):
                act.wait_ge(kv_stat, g + 1)
                A(chain_rs[:, 0:TOK], G[:, g, :], ACT.Ln, bias=eps[:, 0:1], scale=1.0 / HD).then_inc(kv_ln, 1)
                act.wait_ge(kv_ln, g + 1)
                A(chain_rs[:, 0:TOK], chain_rs[:, 0:TOK], ACT.Exp, scale=-0.5).then_inc(kv_rs, 1)

            for g in range(KV):
                for m in range(POINTS):
                    if g and m == 0:
                        kv_chain(g - 1)
                    if g and m == 2:
                        kv_rstd(g - 1)
                    if m % 2 == 0:
                        split((g + 1) // 2, (g + 1) % 2, m // 2, kv_loaded(g + 1))

            def q_chain(u, g):
                after(act, tile_done, T_UNIT + 2 * u + 2)
                after(act, q_ok, u)
                act.wait_ge(kv_n, KV)
                act.wait_ge(kv_t, KV)
                bank = 2 * (g % 2) + 1
                A(chain_raw[:, 0:TOK], G[:, bank, :], ACT.Copy).then_inc(q_raw, 1)
                A(chain_sq[:, 0:TOK], G[:, bank, :], ACT.Square).then_inc(q_raw, 1)

            def q_rstd(u, g):
                bank = 2 * (g % 2) + 1
                after(act, q_stat, u + 1)
                A(chain_rs[:, 0:TOK], G[:, bank, :], ACT.Ln, bias=eps[:, 0:1], scale=1.0 / HD).then_inc(q_ln, 1)
                after(act, q_ln, u + 1)
                A(chain_rs[:, 0:TOK], chain_rs[:, 0:TOK], ACT.Exp, scale=-0.5).then_inc(q_rs, 1)

            def swa_step(u, g, m):
                if m == 0:
                    q_chain(u, g)
                if m == 1:
                    q_rstd(u, g)
                if 0 <= m - 4 < 8:
                    n = m - 4
                    width = P if n < 2 else 2 * P
                    after(act, a_neg, 8 * u + n + 1)
                    after(act, a_t, 8 * u + n - 3)
                    A(p1[:, n % 4, 0:width], sc1[:, n % 3, 0:width], ACT.Exp, bias=st1[:, n, 0:1], scale=-1.0,
                      accum_out=st1[:, n, 1:2]).then_inc(a_exp, 1)
                    after(act, sinku_ok, u + 1)
                    A(st1[:, n, 2:3], sink_u[:, g % 2, 1, n % 2:n % 2 + 1], ACT.Exp,
                      bias=st1[:, n, 0:1]).then_inc(a_es, 1)
                if 0 <= m - 6 < 8:
                    n = m - 6
                    width = P if n < 2 else 2 * P
                    after(act, a_t, 8 * u + n + 1)
                    after(act, a_pv, 8 * u + n - 2)
                    A(pT1[:, n % 3, 0:width], T[:, 0:width], ACT.Copy).then_inc(a_pT, 1)

            def gate_chain(u, g):
                after(act, tile_done, T_UNIT + 2 * u + 1)
                after(act, g_ok, u)
                A(gate_e[:, :], G[:, 2 * (g % 2), :], ACT.Exp, scale=-1.0).then_inc(g_act, 1)
                A(gate_raw[:, :], G[:, 2 * (g % 2), :], ACT.Copy).then_inc(g_act, 1)

            def swa_window(i, g, attend):
                u = 4 * i + g
                for m in range(16):
                    if attend:
                        swa_step(u - 1, window(i, g)[1], m)
                    elif m == 0:
                        kv_chain(KV - 1)
                    elif m == 2:
                        kv_rstd(KV - 1)
                    if m % 2 == 0:
                        split(T_UNIT // 2 + u + m // 8, 1 - m // 8, m % 8 // 2, unit_loaded(u + m // 8, 1 - m // 8))
                    if m == 9:
                        gate_chain(u, g)

            for g in range(KV):
                swa_window(0, g, attend=g > 0)
            with act.Fori(1, UNITS) as i:
                for g in range(KV):
                    swa_window(i, g, attend=True)
            for m in range(16):
                swa_step(4 * UNITS - 1, 3, m)

            def out_block(first, base, loads, attention_over):
                act.wait_ge(tile_done, first)
                attention_over()
                for c in range(KC):
                    A(xh[:, c, META:ALL], mixed[:, c, :], ACT.Copy).then_inc(split_hi, 1)

                def tile(i, half, last=False):
                    c = 2 * i + half
                    if not last:
                        for quarter in range(4):
                            split(first // 2 + i + half, 1 - half, quarter, out_loaded(loads, i + half, 1 - half))
                    act.wait_ge(tile_done, first + c + 1)
                    after(act, y_t, base + c - 1)
                    A((chain_rs if half else y_col)[:, 0:TOK], G[:, half, :], ACT.Copy).then_inc(y_raw, 1)

                for half in range(2):
                    tile(0, half)
                with act.Fori(1, KC // 2 - 1) as i:
                    for half in range(2):
                        tile(i, half)
                tile(KC // 2 - 1, 0)
                tile(KC // 2 - 1, 1, last=True)

            out_block(T_OUT1, 0, OUT1_LOADS, lambda: act.wait_ge(a_out, 4 * UNITS))

            for quarter in range(4):
                split(T_HEAD // 2, 0, quarter, head_loaded(0, 0))
            row_sums(1)
            normalised_hi(1)
            act.wait_ge(lam_mid, 2)
            A(lam[:, 2:4], lam[:, 0:2], ACT.Exp).then_inc(lam_mid, 1)
            act.wait_ge(m_in, 16 * 8)
            for n, m in enumerate((ident, strict[:, :], neg_tri, neg_ones)):
                A(exact[:, n, :], m, ACT.Copy).then_inc(exact_ok, 1)
            act.wait_ge(meta_f, 1)
            A(xh[:, :, 0:META], later[:, 0:META * KC].rearrange("p (c m) -> p c m", c=KC), ACT.Copy).then_inc(meta_hi, 1)

            def copy_out(dst, two, s):
                for b, (a, e) in zip(two, ((0, ALL // 2), (ALL // 2, ALL))):
                    last = A(dst[:, a:e], G[:, b, 0:ALL // 2], ACT.Copy)
                last.then_inc(s, 1)

            def finish(h, ti, p):
                name, _, two, _ = TILES2[ti]
                if p == 0:
                    after(act, tile_done, T_HEAD + 8 * h + ti + 1)
                if name in ("dfq", "dfk"):
                    count = 2 * h + ti + 1
                    if p == 0:
                        after(act, v_t, 2 * h)
                        after(act, d_out, h)
                        after(act, used["dfq"] if ti else used["dfk"], h + ti)
                        for b, (a, e) in zip(two, ((0, TOK),) if ti == 0 else ((0, ALL // 2), (ALL // 2, ALL))):
                            A(chain_raw[:, a:e], G[:, b, 0:e - a], ACT.Copy)
                            last = A(chain_sq[:, a:e], G[:, b, 0:e - a], ACT.Square)
                        last.then_inc(n_raw, 1)
                    if p == 2:
                        after(act, n_stat, count)
                        for b, (a, e) in zip(two, ((0, TOK),) if ti == 0 else ((0, ALL // 2), (ALL // 2, ALL))):
                            last = A(chain_rs[:, a:e], G[:, b, 0:e - a], ACT.Ln, bias=eps[:, 0:1], scale=1.0 / HD)
                        last.then_inc(n_ln, 1)
                        after(act, n_ln, count)
                        width = TOK if ti == 0 else ALL
                        A(chain_rs[:, 0:width], chain_rs[:, 0:width], ACT.Exp, scale=-0.5).then_inc(n_rs, 1)
                if name in ("dfv", "sbv"):
                    n = 1 if name == "dfv" else 2
                    if p == 0:
                        after(act, used["dfk"], h + 1)
                        after(act, v_t, 2 * h + n - 1)
                        copy_out(chain_raw, two, v_raw)
                    if p == 2:
                        after(act, v_t, 2 * h + n)
                        if name == "dfv":
                            after(act, d_pvm, h)
                        else:
                            after(act, b_pv, 5 * h)
                        rows_v, meta_v = (dfv, dfvm) if name == "dfv" else (sbv, sbvm)
                        A(rows_v[:, :, :], G[:, two[0], :].rearrange("p (t n) -> p t n", t=NB), ACT.Copy)
                        A(meta_v[:, :], G[0:META, two[1], 0:P], ACT.Copy).then_inc(used[name], 1)
                if name in ("dfg", "sbg") and p == 0:
                    after(act, used["sbg" if name == "dfg" else "dfg"], h if name == "dfg" else h + 1)
                    A(gate_e[:, :], G[:, two[0], :], ACT.Exp, scale=-1.0).then_inc(e_gate, 1)
                if name == "sbq" and p == 0:
                    after(act, b_z, 5 * h)
                    A(sbq[:, :], G[:, two[0], :], ACT.Copy, scale=SBH ** -0.5).then_inc(used["sbq"], 1)
                if name == "sbk" and p == 0:
                    after(act, b_z, 5 * h)
                    copy_out(sbk, two, used["sbk"])

            def df_step(h, m):
                if m in DF_EXP:
                    n = DF_EXP[m]
                    j = n // 2
                    width = META + P * (j + 1)
                    after(act, d_neg, 8 * h + n + 1)
                    after(act, d_w, 4 * h + j)
                    if n < 2:
                        after(act, b_pv, 5 * h)
                    A(prob[:, n % 2, 0:width], work[:, n % 2, 0:width], ACT.Exp, bias=st2[:, 1, n:n + 1], scale=-1.0,
                      accum_out=st2[:, 2, n:n + 1]).then_inc(d_exp, 1)
                if m in DF_PT:
                    j = DF_PT[m]
                    after(act, d_t, 4 * h + j + 1)
                    after(act, d_pv, 4 * h + j)
                    if j == 0:
                        after(act, d_pvm, h)
                    A(pT2[:, 0:P * (j + 1)], T[:, 0:P * (j + 1)], ACT.Copy).then_inc(d_pT, 1)
                if m == 23:
                    after(act, d_tm, h + 1)
                    after(act, d_pv, 4 * h + NB)
                    A(pT2[0:META, :], T[0:META, :], ACT.Copy).then_inc(d_ptm, 1)
                if m == 25:
                    after(act, d_pvm, h + 1)
                    after(act, used["dfk"], h + 1)
                    A(chain_sq[:, 0:TOK], O[:, :], ACT.Square).then_inc(d_sq, 1)
                if m == 28:
                    after(act, d_stat, h + 1)
                    A(chain_rs[:, 0:TOK], T[:, :], ACT.Ln, bias=eps[:, 1:2], scale=1.0 / P).then_inc(d_ln, 1)
                    after(act, d_ln, h + 1)
                    A(chain_rs[:, 0:TOK], chain_rs[:, 0:TOK], ACT.Exp, scale=-0.5).then_inc(d_rs, 1)

            def sb_step(h, m):
                if m in SB_Z:
                    n = SB_Z[m]
                    size, _, q = sb_tile(n)
                    z, e = S[0:size, n % 2, 0:TOK - q], wts[0:size, n % 2, 0:TOK - q]
                    after(act, b_z, 5 * h + n + 1)
                    if n >= 2:
                        after(act, b_lk, 5 * h + n - 1)
                    else:
                        after(act, d_tm, h + 1)
                    A(e, z, ACT.Abs).then_inc(b_abs, 1)
                    after(act, b_abs, 5 * h + n + 1)
                    A(e, e, ACT.Exp, scale=-1.0).then_inc(b_e, 1)
                    after(act, b_e, 5 * h + n + 1)
                    A(e, e, ACT.Ln, bias=1.0).then_inc(b_ln, 1)
                if m in SB_A:
                    n = SB_A[m]
                    size, _, q = sb_tile(n)
                    after(act, b_c, 5 * h + n + 1)
                    if n >= 2:
                        after(act, b_pv, 5 * h + n - 1)
                    else:
                        after(act, d_w, 4 * h + NB)
                    A(prob[0:size, n % 2, 0:TOK - q], S[0:size, n % 2, 0:TOK - q], ACT.Exp).then_inc(b_a, 1)
                if m in SB_SPLIT:
                    n = SB_SPLIT[m]
                    size, _, q = sb_tile(n)
                    after(act, b_lk, 5 * h + n + 1)
                    after(act, b_c, 5 * h + n)
                    A(lk_h[0:size, 0:TOK - q], work[0:size, n % 2, 0:TOK - q], ACT.Copy).then_inc(b_kh, 1)
                if m in SB_LATER:
                    n = SB_LATER[m]
                    _, _, q = sb_tile(n + 1)
                    after(act, b_sum, 4 * h + n + 1)
                    A(later_h[:, q:TOK], later[:, q:TOK], ACT.Copy).then_inc(b_lh, 1)

            def head(h, attend):
                for ti in range(len(TILES2)):
                    for p in range(POINTS):
                        if ti:
                            finish(h, ti - 1, p)
                        if ti >= 4:
                            df_step(h, 8 * (ti - 4) + p)
                        elif attend:
                            sb_step(h - 1, 8 * ti + p)
                        if p % 2 == 0:
                            split(T_HEAD // 2 + 4 * h + (ti + 1) // 2, (ti + 1) % 2, p // 2, head_loaded(h, ti + 1))
                finish(h, len(TILES2) - 1, 0)

            head(0, attend=False)
            with act.Fori(1, N2) as h:
                head(h, attend=True)
            for m in range(32):
                sb_step(N2 - 1, m)

            def heads_over():
                act.wait_ge(d_out, N2)
                act.wait_ge(b_out, N2)

            out_block(T_OUT2, KC, OUT2_LOADS, heads_over)

        @block.vector
        def _(dve):
            V = nc.vector

            def split(pair, slot, quarter):
                dve.wait_ge(w_hi, 4 * (2 * pair + slot) + quarter + 1)
                q = slice(QTR * quarter, QTR * quarter + QTR)
                V.tensor_tensor(wl[:, slot, q, :], raw[:, slot, q, :], wh[:, slot, q, :].bitcast(F32),
                                ALU.subtract).then_inc(w_lo, 1)

            V.memset(ssq[:, :, :], 1.0)
            V.memset(eps[:, 0:1], EPS)
            V.memset(eps[:, 1:2], SUBLN_EPS).then_inc(sets_ok, 1)

            def scale_rows(layer):
                for t in range(NB):
                    dve.wait_ge(rs_done, 2 * (NB * layer + t) + 2)
                    V.tensor_scalar(rows[:, t, :], rows[:, t, :], rstd[:, layer, t:t + 1], None,
                                    ALU.mult).then_inc(rows_done, 1)

            def normalised_lo(layer):
                for c in range(KC):
                    dve.wait_ge(x_hi, KC * layer + c + 1)
                    V.scalar_tensor_tensor(out=xl[:, c, META:ALL], in0=S[:, c % 2, :], scalar=gnorm[:, layer, c:c + 1],
                                           in1=xh[:, c, META:ALL].bitcast(F32), op0=ALU.mult,
                                           op1=ALU.subtract).then_inc(x_lo, 1)

            scale_rows(0)
            dve.wait_ge(mats_in, 16 * 2)
            normalised_lo(0)
            for quarter in range(4):
                split(0, 0, quarter)
            dve.wait_ge(c_in, 16 * 13)
            V.tensor_scalar(gains[:, 2:3], gains[:, 2:3], HD ** -0.5, None, ALU.mult)
            V.tensor_scalar(gains[:, 4:5], gains[:, 4:5], 1.0 - LAM_INIT, None, ALU.mult)
            V.tensor_scalar(sink[:, 0, :], sink[:, 1, :], -1.0, None, ALU.mult).then_inc(sink_ok, 1)
            dve.wait_ge(rel_mm, 1)
            V.scalar_tensor_tensor(out=relb[:, :], in0=T[0:HEADS, 0:REL_COLS], scalar=HD ** 0.5, in1=relc[:, 1, :],
                                   op0=ALU.mult, op1=ALU.add).then_inc(rel_ok, 1)

            def kv_finish(g):
                dve.wait_ge(kv_rs, g + 1)
                V.scalar_tensor_tensor(out=kT1[0:HD, g, :], in0=chain_raw[0:HD, 0:TOK], scalar=gains[0:HD, 1:2],
                                       in1=chain_rs[0:HD, 0:TOK], op0=ALU.mult, op1=ALU.mult).then_inc(kv_n, 1)
                dve.wait_ge(kv_t, g + 1)
                V.tensor_copy(v1[:, g, :, :], T[:, :].rearrange("p (t n) -> p t n", t=NB)[:, :, HD:P]).then_inc(kv_v, 1)

            for g in range(KV):
                for m in range(POINTS):
                    if g and m == 3:
                        kv_finish(g - 1)
                    if m % 2 == 0:
                        split((g + 1) // 2, (g + 1) % 2, m // 2)

            def swa_step(i, u, g, m):
                if m == 2:
                    after(dve, q_rs, u + 1)
                    V.scalar_tensor_tensor(out=qn[:, :], in0=chain_raw[:, 0:TOK], scalar=gains[:, 0:1],
                                           in1=chain_rs[:, 0:TOK], op0=ALU.mult, op1=ALU.mult).then_inc(q_ok, 1)
                if 0 <= m - 3 < 8:
                    n = m - 3
                    width = P if n < 2 else 2 * P
                    if n == 0:
                        after(dve, bias_in[g % 2], 16 * (2 * i + g // 2 + 1))
                        after(dve, sinku_ok, u + 1)
                    after(dve, a_exp, 8 * u + n - 2)
                    after(dve, a_s, 8 * u + n + 1)
                    V.tensor_copy(st1[:, n, 5:6], sink_u[:, g % 2, 0, n % 2:n % 2 + 1])
                    V.tensor_tensor_reduce(sc1[:, n % 3, 0:width], S[:, n % 2, 0:width],
                                           bias[:, g % 2, n % 2, 2 * P - width:2 * P], -HD ** -0.5,
                                           sink_u[:, g % 2, 0, n % 2:n % 2 + 1], ALU.add, ALU.min,
                                           st1[:, n, 0:1]).then_inc(a_neg, 1)
                if 0 <= m - 5 < 8:
                    n = m - 5
                    width = P if n < 2 else 2 * P
                    after(dve, a_es, 8 * u + n + 1)
                    V.tensor_tensor(st1[:, n, 3:4], st1[:, n, 1:2], st1[:, n, 2:3], ALU.add).then_inc(a_mid, 1)
                    after(dve, a_mid, 16 * u + 2 * n + 1)
                    V.reciprocal(st1[:, n, 4:5], st1[:, n, 3:4]).then_inc(a_mid, 1)
                    after(dve, a_mid, 16 * u + 2 * n + 2)
                    V.tensor_scalar(p1[:, n % 4, 0:width], p1[:, n % 4, 0:width], st1[:, n, 4:5], None,
                                    ALU.mult).then_inc(a_p, 1)
                if m == 15:
                    after(dve, a_pv, 8 * u + 8)
                    after(dve, g_ok, u + 1)
                    V.tensor_tensor(mixed[:, ds(4 * g + i, 1), :].rearrange("p a n -> p (a n)"), O[:, :], sg1[:, :],
                                    ALU.mult).then_inc(a_out, 1)

            def gate_finish(u):
                after(dve, g_act, 2 * u + 2)
                after(dve, a_out, u)
                V.tensor_scalar(gate_e[:, :], gate_e[:, :], 1.0, None, ALU.add).then_inc(g_mid, 1)
                after(dve, g_mid, 2 * u + 1)
                V.reciprocal(gate_e[:, :], gate_e[:, :]).then_inc(g_mid, 1)
                after(dve, g_mid, 2 * u + 2)
                V.tensor_tensor(sg1[:, :], gate_raw[:, :], gate_e[:, :], ALU.mult).then_inc(g_ok, 1)

            def swa_window(i, g, attend):
                u = 4 * i + g
                ip, gp = window(i, g)
                for m in range(16):
                    if attend:
                        swa_step(ip, u - 1, gp, m)
                    elif m == 3:
                        kv_finish(KV - 1)
                    if m % 2 == 0:
                        split(T_UNIT // 2 + u + m // 8, 1 - m // 8, m % 8 // 2)
                gate_finish(u)

            for g in range(KV):
                swa_window(0, g, attend=g > 0)
            with dve.Fori(1, UNITS) as i:
                for g in range(KV):
                    swa_window(i, g, attend=True)
            for m in range(16):
                swa_step(UNITS - 1, 4 * UNITS - 1, 3, m)

            def out_block(first, base):
                for c in range(KC):
                    dve.wait_ge(split_hi, base + c + 1)
                    V.tensor_tensor(xl[:, c, META:ALL], mixed[:, c, :], xh[:, c, META:ALL].bitcast(F32),
                                    ALU.subtract).then_inc(split_lo, 1)

                def add(i, half):
                    c = 2 * i + half
                    res, dst = (chain_sq, gate_raw) if half else (chain_raw, gate_e)
                    dve.wait_ge(y_t, base + c + 1)
                    dve.wait_ge(y_in[half], 8 * base + 16 * (i + 1))
                    if base:
                        after(dve, y_out[half], 8 * base + 16 * i)
                        V.tensor_tensor(dst[:, 0:TOK], T[:, :], res[:, 0:TOK], ALU.add).then_inc(y_sum, 1)
                    else:
                        V.tensor_tensor(rows[:, :, ds(P * c, P)], T[:, :].rearrange("p (t n) -> p t n", t=NB),
                                        res[:, 0:TOK].rearrange("p (t n) -> p t n", t=NB), ALU.add).then_inc(y_sum, 1)

                def tile(i, half, last=False):
                    if not last:
                        for quarter in range(4):
                            split(first // 2 + i + half, 1 - half, quarter)
                    if half:
                        add(i, 0)
                    elif not (isinstance(i, int) and i == 0):
                        add(i - 1, 1)

                for half in range(2):
                    tile(0, half)
                with dve.Fori(1, KC // 2 - 1) as i:
                    for half in range(2):
                        tile(i, half)
                tile(KC // 2 - 1, 0)
                tile(KC // 2 - 1, 1, last=True)
                add(KC // 2 - 1, 1)

            out_block(T_OUT1, 0)

            for quarter in range(4):
                split(T_HEAD // 2, 0, quarter)
            for half in range(2):
                dve.wait_ge(y_out[half], 16 * (KC // 2))
            scale_rows(1)
            dve.wait_ge(rs_done, 2 * (2 * NB + 1))
            V.tensor_scalar(metar, metar, rstd[0:META, 1, NB:NB + 1], None, ALU.mult).then_inc(meta_rows, 1)
            normalised_lo(1)
            for n in range(2):
                V.tensor_tensor_reduce(lamv[:, 2 * n, :], lamv[:, 2 * n, :], lamv[:, 2 * n + 1, :], 1.0, 0.0,
                                       ALU.mult, ALU.add, lam[:, n:n + 1]).then_inc(lam_mid, 1)
            dve.wait_ge(lam_mid, 3)
            V.scalar_tensor_tensor(out=lam[:, 4:5], in0=lam[:, 3:4], scalar=LAM_INIT, in1=lam[:, 2:3],
                                   op0=ALU.subtract, op1=ALU.subtract).then_inc(lam_ok, 1)
            dve.wait_ge(meta_t, 1)
            meta_cols = later[:, 0:META * KC].rearrange("p (c m) -> p c m", c=KC)
            V.tensor_tensor(meta_cols, T[:, 0:META * KC].rearrange("p (c m) -> p c m", c=KC),
                            gnorm[:, 1, :].rearrange("p (c a) -> p c a", a=1).broadcast_to([P, KC, META]),
                            ALU.mult).then_inc(meta_f, 1)
            dve.wait_ge(meta_hi, 1)
            V.tensor_tensor(xl[:, :, 0:META], meta_cols, xh[:, :, 0:META].bitcast(F32), ALU.subtract).then_inc(meta_lo, 1)

            def finish(h, ti, p):
                name, _, two, _ = TILES2[ti]
                if name in ("dfq", "dfk"):
                    count = 2 * h + ti + 1
                    buf = dfk if ti else dfq
                    width = ALL if ti else TOK
                    if p == 3:
                        after(dve, n_rs, count)
                        V.scalar_tensor_tensor(out=buf[:, :], in0=chain_raw[:, 0:width], scalar=gains[:, 2 + ti:3 + ti],
                                               in1=chain_rs[:, 0:width], op0=ALU.mult, op1=ALU.mult).then_inc(n_kn, 1)
                    if p == 6:
                        after(dve, n_rot, count)
                        if ti:
                            g_v = G[:, two[0]:two[1] + 1, 0:ALL // 2]
                            v = lambda b: b.rearrange("p (a n) -> p a n", a=2)
                            V.tensor_tensor(v(chain_sq[:, :]), g_v, v(rope[:, 1, :]), ALU.mult).then_inc(n_mid, 1)
                        else:
                            V.tensor_tensor(chain_sq[:, 0:TOK], G[:, two[0], :], rope[:, 1, META:ALL],
                                            ALU.mult).then_inc(n_mid, 1)
                        V.tensor_tensor(buf[:, :], buf[:, :], rope[:, 0, ALL - width:ALL], ALU.mult).then_inc(n_mid, 1)
                        after(dve, n_mid, 2 * count)
                        V.tensor_tensor(buf[:, :], buf[:, :], chain_sq[:, 0:width], ALU.add).then_inc(used[name], 1)
                if name in ("dfg", "sbg") and p == 0:
                    n = 2 * h + (1 if name == "dfg" else 2)
                    after(dve, e_gate, n)
                    V.tensor_scalar(gate_e[:, :], gate_e[:, :], 1.0, None, ALU.add).then_inc(m_gate, 1)
                    after(dve, m_gate, 2 * n - 1)
                    V.reciprocal(gate_e[:, :], gate_e[:, :]).then_inc(m_gate, 1)
                    after(dve, m_gate, 2 * n)
                    V.tensor_tensor((dsg if name == "dfg" else ssg)[:, :], G[:, two[0], :], gate_e[:, :],
                                    ALU.mult).then_inc(used[name], 1)

            def df_step(h, m):
                if m == 0:
                    after(dve, d_sm, 2 * h + 2)
                    V.tensor_scalar(smeta[:, :, :], T[:, 0:2 * NB * META].rearrange("p (n m) -> p n m", m=META), -1.0,
                                    None, ALU.mult).then_inc(d_smn, 1)
                    after(dve, d_smn, h + 1)
                    V.tensor_reduce(st2[:, 0, :], smeta[:, :, :], AX_X, ALU.min).then_inc(d_min, 1)
                if m in DF_S:
                    n = DF_S[m]
                    width = P * (n // 2 + 1)
                    after(dve, d_exp, 8 * h + n - 1)
                    if n == 0:
                        after(dve, d_min, h + 1)
                    after(dve, d_s, 8 * h + n + 1)
                    V.tensor_copy(work[:, n % 2, 0:META], smeta[:, n, :])
                    V.tensor_tensor_reduce(work[:, n % 2, META:META + width], S[:, n % 2, 0:width],
                                           causal[:, ALL - width:ALL], -1.0, st2[:, 0, n:n + 1], ALU.add, ALU.min,
                                           st2[:, 1, n:n + 1]).then_inc(d_neg, 1)
                if m in DF_W:
                    j = DF_W[m]
                    width = META + P * (j + 1)
                    done = 16 * h + 4 * j
                    after(dve, d_exp, 8 * h + 2 * j + 2)
                    V.reciprocal(st2[:, 3, 2 * j:2 * j + 2], st2[:, 2, 2 * j:2 * j + 2]).then_inc(d_mid, 1)
                    after(dve, d_mid, done + 1)
                    V.tensor_tensor(st2[:, 3, 2 * j + 1:2 * j + 2], st2[:, 3, 2 * j + 1:2 * j + 2], lam[:, 4:5],
                                    ALU.mult).then_inc(d_mid, 1)
                    after(dve, d_mid, done + 2)
                    V.tensor_scalar(prob[:, 1, 0:width], prob[:, 1, 0:width], st2[:, 3, 2 * j + 1:2 * j + 2], None,
                                    ALU.mult).then_inc(d_mid, 1)
                    after(dve, d_mid, done + 3)
                    after(dve, d_t, 4 * h + j - 1)
                    V.scalar_tensor_tensor(out=wts[:, j % 2, 0:width], in0=prob[:, 0, 0:width],
                                           scalar=st2[:, 3, 2 * j:2 * j + 1], in1=prob[:, 1, 0:width], op0=ALU.mult,
                                           op1=ALU.add).then_inc(d_mid, 1)
                    after(dve, d_mid, done + 4)
                    V.tensor_copy(wmeta[:, j, :], wts[:, j % 2, 0:META]).then_inc(d_w, 1)
                if m == 29:
                    after(dve, d_rs, h + 1)
                    V.scalar_tensor_tensor(out=chain_sq[:, 0:TOK], in0=O[:, :], scalar=gains[:, 4:5],
                                           in1=chain_rs[:, 0:TOK], op0=ALU.mult, op1=ALU.mult).then_inc(d_norm, 1)
                    after(dve, d_norm, h + 1)
                    V.tensor_tensor(mixed[:, ds(N2 + h, 1), :].rearrange("p a n -> p (a n)"), chain_sq[:, 0:TOK],
                                    dsg[:, :], ALU.mult).then_inc(d_out, 1)

            def sb_step(h, m):
                if m == 0:
                    V.memset(later[:, :], 0.0).then_inc(b_zero, 1)
                if m in SB_A and SB_A[m] < NB:
                    n = SB_A[m]
                    _, _, q = sb_tile(n)
                    after(dve, b_c, 5 * h + n + 1)
                    if n:
                        after(dve, b_sum, 4 * h + n)
                    else:
                        after(dve, b_zero, h + 1)
                    V.tensor_tensor(later[:, q:TOK], later[:, q:TOK], work[:, n % 2, 0:TOK - q], ALU.add).then_inc(b_sum, 1)
                if m in SB_LK:
                    n = SB_LK[m]
                    size, _, q = sb_tile(n)
                    lk = work[0:size, n % 2, 0:TOK - q]
                    after(dve, b_ln, 5 * h + n + 1)
                    if n >= 2:
                        after(dve, b_c, 5 * h + n - 1)
                    mm = V.scalar_tensor_tensor(out=lk, in0=S[0:size, n % 2, 0:TOK - q], scalar=0.0,
                                                in1=wts[0:size, n % 2, 0:TOK - q], op0=ALU.max, op1=ALU.add)
                    if n < NB:
                        mm.then_inc(b_sp, 1)
                        after(dve, b_sp, 4 * h + n + 1)
                        V.tensor_tensor(work[:, n % 2, 0:P], work[:, n % 2, 0:P], before, ALU.mult).then_inc(b_lk, 1)
                    else:
                        mm.then_inc(b_lk, 1)
                if m in SB_SPLIT:
                    n = SB_SPLIT[m]
                    size, _, q = sb_tile(n)
                    after(dve, b_kh, 5 * h + n + 1)
                    V.tensor_tensor(lk_l[0:size, 0:TOK - q], work[0:size, n % 2, 0:TOK - q],
                                    lk_h[0:size, 0:TOK - q].bitcast(F32), ALU.subtract).then_inc(b_kl, 1)
                if m in SB_LATER:
                    n = SB_LATER[m]
                    _, _, q = sb_tile(n + 1)
                    after(dve, b_lh, 4 * h + n + 1)
                    V.tensor_tensor(later_l[:, q:TOK], later[:, q:TOK], later_h[:, q:TOK].bitcast(F32),
                                    ALU.subtract).then_inc(b_ll, 1)
                if m == 27:
                    after(dve, b_pv, 5 * h + 5)
                    V.tensor_tensor(mixed[:, ds(h, 1), :].rearrange("p a n -> p (a n)"), O[:, :], ssg[:, :],
                                    ALU.mult).then_inc(b_out, 1)

            def head(h, attend):
                for ti in range(len(TILES2)):
                    for p in range(POINTS):
                        if ti:
                            finish(h, ti - 1, p)
                        if ti >= 4:
                            df_step(h, 8 * (ti - 4) + p)
                        elif attend:
                            sb_step(h - 1, 8 * ti + p)
                        if p % 2 == 0:
                            split(T_HEAD // 2 + 4 * h + (ti + 1) // 2, (ti + 1) % 2, p // 2)
                finish(h, len(TILES2) - 1, 0)

            dve.wait_ge(m_in, 16 * 8)
            dve.wait_ge(lam_ok, 1)
            head(0, attend=False)
            with dve.Fori(1, N2) as h:
                head(h, attend=True)
            for m in range(32):
                sb_step(N2 - 1, m)
            out_block(T_OUT2, KC)


INPUTS = {"x": None, "rel_bias": None, "swa_norm": 0, "swa_w_in": 0, "swa_q_gain": 0, "swa_k_gain": 0, "swa_sinks": 0,
          "swa_w_out": 0, "meta_2": None, "norm_w_2": 0, "w_in_2": 0, "q_norm_w_2": 0, "k_norm_w_2": 0,
          "lambda_q1_2": 0, "lambda_k1_2": 0, "lambda_q2_2": 0, "lambda_k2_2": 0, "subln_w_2": 0, "w_out_2": 0}


def kernel(**inputs):
    from concourse import bacc
    from concourse.bass_utils import run_bass_kernel_spmd

    nc = bacc.Bacc("TRN2", target_bir_lowering=False, num_devices=1)
    arrays, args = {}, []
    for name in INPUTS:
        a = np.ascontiguousarray(inputs[name])
        if name == "x" or INPUTS[name] is not None:
            a = a.reshape(a.shape[1:])
        arrays[f"in_{name}"] = a
    arrays.update({name: np.ascontiguousarray(a) for name, a in shape_constants().items()})
    for name, a in arrays.items():
        args.append(nc.dram_tensor(name, a.shape, mybir.dt.from_np(a.dtype), kind="ExternalInput").ap())
    args.append(nc.dram_tensor("rel_rows", (HEADS * P + 1, REL_PITCH), F32, kind="Internal").ap())
    args.append(nc.dram_tensor("x1", (TOK, D), F32, kind="Internal").ap())
    args.append(nc.dram_tensor("out", (TOK, D), F32, kind="ExternalOutput").ap())
    build(nc, *args)
    result = run_bass_kernel_spmd(nc, [arrays], core_ids=[0])
    return result.results[0]["out"].reshape(1, TOK, D)
```
